# Optimizing a Trainium2 kernel written in Bass

```python
import jax, jax.numpy as jnp
from jax import lax
import numpy as np

D_MODEL = 1024
BATCH = 1
SEQ = 512
DEPTH = 1
DEC_BATCH = 1
DEC_SEQ = 32
PAST_LEN = 256

CHUNK = 64
RET_HEADS = 4
RET_HEAD_DIM = 128
RET_WIDTH = RET_HEADS * RET_HEAD_DIM
CONV_WIDTH = D_MODEL - RET_WIDTH
MIX_WIDTH = RET_WIDTH + CONV_WIDTH
IN_WIDTH = 4 * RET_WIDTH + 2 * CONV_WIDTH
CONV_KERNEL = 31
ROPE_BASE = 10000.0
PEER_HEADS = 8
PEER_KEYS = 128
PEER_EXPERTS = PEER_KEYS * PEER_KEYS
PEER_TOPK = 16
PEER_KEY_DIM = 128
PEER_BLOCK = 256
EPS = 1e-6

kernel_name = 'retention_conformer_peer_stream'

def _rmsnorm(x, gain):
    xf = x.astype(jnp.float32)
    y = xf * lax.rsqrt(jnp.mean(xf * xf, axis=-1, keepdims=True) + EPS)
    return (y * gain.astype(jnp.float32)).astype(x.dtype)

def _rotary(t, pos):
    half = t.shape[-1] // 2
    inv_freq = ROPE_BASE ** (-jnp.arange(half, dtype=jnp.float32) / half)
    ang = pos[:, None] * inv_freq[None, :]
    cos, sin = jnp.cos(ang), jnp.sin(ang)
    t1, t2 = t[..., :half], t[..., half:]
    return jnp.concatenate([t1 * cos - t2 * sin, t1 * sin + t2 * cos], axis=-1)

def _retention_decays():
    return jnp.log1p(-jnp.exp2(-5.0 - jnp.arange(RET_HEADS, dtype=jnp.float32)))

def _retention_block(q, k, v, s, log_gamma):
    L = q.shape[2]
    idx = jnp.arange(L, dtype=jnp.float32)
    diff = idx[:, None] - idx[None, :]
    causal = diff >= 0
    decay = jnp.where(causal[None], jnp.exp(log_gamma[:, None, None] * jnp.where(causal, diff, 0.0)[None]), 0.0)
    scores = jnp.einsum('bhld,bhmd->bhlm', q, k) * decay[None]
    cross = jnp.exp(log_gamma[:, None] * (idx[None, :] + 1.0))
    out = (jnp.einsum('bhlm,bhme->bhle', scores, v)
           + jnp.einsum('bhld,bhde->bhle', q, s) * cross[None, :, :, None])
    k_w = k * jnp.exp(log_gamma[:, None] * (L - 1.0 - idx[None, :]))[None, :, :, None]
    s_new = jnp.exp(log_gamma * L)[None, :, None, None] * s + jnp.einsum('bhld,bhle->bhde', k_w, v)
    return out, s_new

def _token_mixers(h, pos, ret_state, conv_buf, w_in, ret_gn_gain, conv_dw, conv_dw_bias,
                  conv_ln_gain, conv_ln_bias, w_out):
    B, L, _ = h.shape
    z = h @ w_in
    q, k, v, g, a, b = jnp.split(
        z, [RET_WIDTH, 2 * RET_WIDTH, 3 * RET_WIDTH, 4 * RET_WIDTH, 4 * RET_WIDTH + CONV_WIDTH], axis=-1)

    def heads(t):
        return t.reshape(B, L, RET_HEADS, RET_HEAD_DIM).transpose(0, 2, 1, 3).astype(jnp.float32)
    q = _rotary(heads(q), pos)
    k = _rotary(heads(k), pos) * (RET_HEAD_DIM ** -0.5)
    v = heads(v)
    blk = min(CHUNK, L)
    n_blk = L // blk

    def to_blocks(t):
        return t.reshape(B, RET_HEADS, n_blk, blk, RET_HEAD_DIM).transpose(2, 0, 1, 3, 4)
    log_gamma = _retention_decays()

    def step(s, qkv):
        o_blk, s = _retention_block(qkv[0], qkv[1], qkv[2], s, log_gamma)
        return s, o_blk
    s_new, o = lax.scan(step, ret_state.astype(jnp.float32), (to_blocks(q), to_blocks(k), to_blocks(v)))
    o = o.transpose(1, 2, 0, 3, 4).reshape(B, RET_HEADS, L, RET_HEAD_DIM)
    oc = o - jnp.mean(o, axis=-1, keepdims=True)
    o = oc * lax.rsqrt(jnp.mean(oc * oc, axis=-1, keepdims=True) + EPS)
    o = o.transpose(0, 2, 1, 3).reshape(B, L, RET_WIDTH) * ret_gn_gain.astype(jnp.float32)
    y_ret = jax.nn.silu(g.astype(jnp.float32)) * o

    u = a * jax.nn.sigmoid(b)
    ext = jnp.concatenate([conv_buf.astype(u.dtype), u], axis=1)
    c = lax.conv_general_dilated(ext, conv_dw[:, None, :].astype(u.dtype), window_strides=(1,),
                                 padding='VALID', dimension_numbers=('NWC', 'WIO', 'NWC'),
                                 feature_group_count=CONV_WIDTH)
    c = c.astype(jnp.float32) + conv_dw_bias.astype(jnp.float32)
    cm = c - jnp.mean(c, axis=-1, keepdims=True)
    c = (cm * lax.rsqrt(jnp.mean(cm * cm, axis=-1, keepdims=True) + EPS)
         * conv_ln_gain.astype(jnp.float32) + conv_ln_bias.astype(jnp.float32))
    y_conv = jax.nn.silu(c)

    y = jnp.concatenate([y_ret, y_conv], axis=-1).astype(h.dtype) @ w_out
    new_buf = ext[:, ext.shape[1] - (CONV_KERNEL - 1):]
    return y, s_new.astype(h.dtype), new_buf

def _peer(x2d, peer_query, peer_sub_keys, peer_down, peer_up):
    T, D = x2d.shape
    n_blocks = -(-T // PEER_BLOCK)
    xp = jnp.pad(x2d, ((0, n_blocks * PEER_BLOCK - T), (0, 0)))
    keys = peer_sub_keys.astype(jnp.float32)

    def block(xb):
        P = xb.shape[0]
        qry = (xb @ peer_query).reshape(P, PEER_HEADS, 2, PEER_KEY_DIM).astype(jnp.float32)
        scores = jnp.einsum('phsd,hsnd->phsn', qry, keys)
        top_s, top_i = lax.top_k(scores, PEER_TOPK)
        cand = top_s[:, :, 0, :, None] + top_s[:, :, 1, None, :]
        best_s, best_c = lax.top_k(cand.reshape(P, PEER_HEADS, PEER_TOPK * PEER_TOPK), PEER_TOPK)
        ia = jnp.take_along_axis(top_i[:, :, 0], best_c // PEER_TOPK, axis=-1)
        ib = jnp.take_along_axis(top_i[:, :, 1], best_c % PEER_TOPK, axis=-1)
        expert = (ia * PEER_KEYS + ib).reshape(P, PEER_HEADS * PEER_TOPK)
        gate = jax.nn.softmax(best_s, axis=-1).reshape(P, PEER_HEADS * PEER_TOPK)
        u_rows = peer_down[expert]
        act = jax.nn.gelu(jnp.einsum('pd,ped->pe', xb, u_rows).astype(jnp.float32))
        v_rows = peer_up[expert]
        return jnp.einsum('pe,ped->pd', (gate * act).astype(xb.dtype), v_rows)

    out = lax.map(block, xp.reshape(n_blocks, PEER_BLOCK, D))
    return out.reshape(n_blocks * PEER_BLOCK, D)[:T]

def _layer(x, pos, ret_state, conv_buf, norm_mix, w_in, ret_gn_gain, conv_dw, conv_dw_bias,
           conv_ln_gain, conv_ln_bias, w_out, norm_ffn, peer_query, peer_sub_keys, peer_down, peer_up):
    y, s_new, buf_new = _token_mixers(_rmsnorm(x, norm_mix), pos, ret_state, conv_buf, w_in, ret_gn_gain,
                                      conv_dw, conv_dw_bias, conv_ln_gain, conv_ln_bias, w_out)
    x = x + y
    h = _rmsnorm(x, norm_ffn)
    x = x + _peer(h.reshape(-1, x.shape[-1]), peer_query, peer_sub_keys, peer_down, peer_up).reshape(x.shape)
    return x, s_new, buf_new

def setup_inputs(seed: int = 0) -> dict:
    key = jax.random.key(seed)
    ks = jax.random.split(key, 20)
    f32 = jnp.float32
    nrm = lambda k, shape, scale: scale * jax.random.normal(k, shape, f32)
    return {
        'x_prompt': nrm(ks[0], (BATCH, SEQ, D_MODEL), 1.0),
        'x_sample': nrm(ks[1], (DEC_BATCH, DEC_SEQ, D_MODEL), 1.0),
        'state_retention': nrm(ks[2], (DEPTH, DEC_BATCH, RET_HEADS, RET_HEAD_DIM, RET_HEAD_DIM), 1.0),
        'state_conv': nrm(ks[3], (DEPTH, DEC_BATCH, CONV_KERNEL - 1, CONV_WIDTH), 0.5),
        'norm_mix': 1.0 + nrm(ks[4], (DEPTH, D_MODEL), 0.02),
        'w_in': nrm(ks[5], (DEPTH, D_MODEL, IN_WIDTH), D_MODEL ** -0.5),
        'ret_gn_gain': 1.0 + nrm(ks[6], (DEPTH, RET_WIDTH), 0.02),
        'conv_dw': nrm(ks[7], (DEPTH, CONV_KERNEL, CONV_WIDTH), CONV_KERNEL ** -0.5),
        'conv_dw_bias': nrm(ks[8], (DEPTH, CONV_WIDTH), 0.02),
        'conv_ln_gain': 1.0 + nrm(ks[9], (DEPTH, CONV_WIDTH), 0.02),
        'conv_ln_bias': nrm(ks[10], (DEPTH, CONV_WIDTH), 0.02),
        'w_out': nrm(ks[11], (DEPTH, MIX_WIDTH, D_MODEL), MIX_WIDTH ** -0.5),
        'norm_ffn': 1.0 + nrm(ks[12], (DEPTH, D_MODEL), 0.02),
        'peer_query': nrm(ks[13], (DEPTH, D_MODEL, PEER_HEADS * 2 * PEER_KEY_DIM), D_MODEL ** -0.5),
        'peer_sub_keys': nrm(ks[14], (DEPTH, PEER_HEADS, 2, PEER_KEYS, PEER_KEY_DIM), PEER_KEY_DIM ** -0.5),
        'peer_down': nrm(ks[15], (DEPTH, PEER_EXPERTS, D_MODEL), D_MODEL ** -0.5),
        'peer_up': nrm(ks[16], (DEPTH, PEER_EXPERTS, D_MODEL), PEER_HEADS ** -0.5),
        'norm_final': 1.0 + nrm(ks[17], (D_MODEL,), 0.02),
    }

def reference(x_prompt, x_sample, state_retention, state_conv, norm_mix, w_in, ret_gn_gain, conv_dw,
              conv_dw_bias, conv_ln_gain, conv_ln_bias, w_out, norm_ffn, peer_query, peer_sub_keys,
              peer_down, peer_up, norm_final):
    bp, lp, _ = x_prompt.shape
    ls = x_sample.shape[1]
    pos_p = jnp.arange(lp, dtype=jnp.float32)
    pos_s = PAST_LEN + jnp.arange(ls, dtype=jnp.float32)
    ret0 = jnp.zeros((bp, RET_HEADS, RET_HEAD_DIM, RET_HEAD_DIM), x_prompt.dtype)
    conv0 = jnp.zeros((bp, CONV_KERNEL - 1, CONV_WIDTH), x_prompt.dtype)
    xp, xs = x_prompt, x_sample
    ret_p, ret_s, conv_p, conv_s = [], [], [], []
    for l in range(DEPTH):
        weights = (norm_mix[l], w_in[l], ret_gn_gain[l], conv_dw[l], conv_dw_bias[l], conv_ln_gain[l],
                   conv_ln_bias[l], w_out[l], norm_ffn[l], peer_query[l], peer_sub_keys[l],
                   peer_down[l], peer_up[l])
        xp, r, c = _layer(xp, pos_p, ret0, conv0, *weights)
        ret_p.append(r)
        conv_p.append(c)
        xs, r, c = _layer(xs, pos_s, state_retention[l], state_conv[l], *weights)
        ret_s.append(r)
        conv_s.append(c)
    y_prompt = _rmsnorm(xp, norm_final)
    y_sample = _rmsnorm(xs, norm_final)
    return (y_prompt, y_sample, jnp.stack(ret_p), jnp.stack(ret_s), jnp.stack(conv_p), jnp.stack(conv_s))


_drawn_inputs = setup_inputs


def setup_inputs(seed=0):
    import zlib

    import numpy as np

    out = dict(_drawn_inputs(seed))
    spreads = {}
    factors = {'ret_gn_gain': 39.269,
     'conv_ln_gain': 35.795,
     'conv_ln_bias': 33.03,
     'norm_final': 24.163,
     'norm_ffn': 17.891}
    for name, (base, spread) in spreads.items():
        noise = np.random.default_rng([zlib.crc32(name.encode()), seed]).standard_normal(out[name].shape)
        drawn = base * np.exp(spread * noise) if base else spread * noise
        out[name] = __import__('jax').numpy.asarray(drawn.astype(out[name].dtype))
    for name, factor in factors.items():
        out[name] = (out[name] * factor).astype(out[name].dtype)
    return out
```

```python
import math
from contextlib import ExitStack

import numpy as np
import concourse.bass as bass
from concourse import mybir

FP32 = mybir.dt.float32
U32 = mybir.dt.uint32
ALU = mybir.AluOpType
ACT = mybir.ActivationFunctionType
AX = mybir.AxisListType

P = 128
D = 1024
KD = D // P
SEQ, DEC = 512, 32
T = SEQ + DEC
TILES = SEQ // P + 1
ROWS = [P] * (SEQ // P) + [DEC]
SAMPLE = TILES - 1
PAST = 256
HEADS, HD = 4, 128
RW = HEADS * HD
CW = D - RW
CT = CW // P
TAPS = 31
PAD = TAPS - 1
SEC = 512
SECTIONS = (4 * RW + 2 * CW + D + 2048) // SEC
S_Q, S_K, S_V, S_G, S_A, S_B, S_OUT, S_QUERY = 0, 1, 2, 3, 4, 5, 6, 8
WEIGHT_ORDER = [S_A, S_B, S_Q, S_K, S_V, S_G, S_OUT, S_OUT + 1] + [S_QUERY + i for i in range(4)]
WSLOTS = 3
PH, KEYS, TOPK = 8, 128, 16
EXPERTS = KEYS * KEYS
SIDES = 2 * PH
FOLDED = P // DEC
VT = (TILES - 1) * PH + PH // FOLDED
EPS = 1e-6
LOWEST = -3.0e38
DSLOTS, USLOTS = 8, 16


def shape_constants():
    f = np.float32
    half = HD // 2
    inv = (f(10000.0) ** (-np.arange(half, dtype=f) / f(half))).astype(f)
    pos = np.concatenate([np.arange(SEQ, dtype=f), f(PAST) + np.arange(DEC, dtype=f)])
    ang = (pos[:, None] * inv[None, :]).astype(f).astype(np.float64)
    trig = np.zeros((P, TILES, 2, half), f)
    for t in range(TILES):
        r = ROWS[t]
        trig[:r, t, 0] = np.cos(ang[t * P:t * P + r])
        trig[:r, t, 1] = np.sin(ang[t * P:t * P + r])
    log_gamma = np.log1p(-np.exp2(-5.0 - np.arange(HEADS)))
    i = np.arange(P)
    diff = i[None, :] - i[:, None]
    scale = HD ** -0.5
    decay = np.zeros((P, HEADS, P), f)
    cross = np.zeros((P, HEADS, P), f)
    key_decay = np.zeros((P, 2, HEADS), f)
    for h in range(HEADS):
        decay[:, h] = np.where(diff >= 0, np.exp(log_gamma[h] * np.maximum(diff, 0)), 0.0) * scale
        cross[:, h] = np.exp(log_gamma[h] * (i + 1.0))[None, :]
        key_decay[:, 0, h] = np.exp(log_gamma[h] * (P - 1.0 - i)) * scale
        key_decay[:DEC, 1, h] = np.exp(log_gamma[h] * (DEC - 1.0 - i[:DEC])) * scale
    ident = np.eye(P, dtype=f)
    fold = (np.arange(P)[:, None] % DEC == np.arange(P)[None, :]).astype(f)
    iota = np.broadcast_to(np.arange(TOPK, dtype=f), (P, TOPK))
    parts = [trig.reshape(P, -1), decay.reshape(P, -1), cross.reshape(P, -1), key_decay.reshape(P, -1),
             ident, fold, iota]
    return np.concatenate(parts, axis=1).astype(f)


C_TRIG = 0
C_DECAY = C_TRIG + TILES * HD
C_CROSS = C_DECAY + HEADS * P
C_KDEC = C_CROSS + HEADS * P
C_IDENT = C_KDEC + 2 * HEADS
C_FOLD = C_IDENT + P
C_IOTA = C_FOLD + P
C_WIDTH = C_IOTA + TOPK
G_MIX = 0
G_RET = G_MIX + KD
G_BIAS = G_RET + HEADS
G_LNG = G_BIAS + CT
G_LNB = G_LNG + CT
G_TAPS = G_LNB + CT
G_WIDTH = G_TAPS + CT * TAPS


def gammas(length):
    return [float(np.exp(np.log1p(-np.exp2(-5.0 - h)) * length)) for h in range(HEADS)]


def psum_jobs():
    jobs = [(("norm_t", t, i), "dve") for t in range(TILES) for i in range(2)]
    for s in (S_A, S_B):
        jobs += [(("glu", s, c), "act") for c in range(CT + 1)]
    for s in (S_Q, S_K, S_V, S_G):
        jobs += [(("qkvg", s, t), "act") for t in range(TILES)]
    jobs += [(("ln_mean", i), "dve") for i in range(2)]
    jobs += [(("ln_var", i), "dve") for i in range(2)]
    for t in range(TILES):
        jobs += [(("ret_qT", t), "dve"), (("ret_kT", t), "dve"), (("ret_scores", t), "dve"),
                 (("ret_out", t), "dve"), (("ret_state", t), "dve"), (("ret_yT", t), "dve")]
    for t in range(TILES):
        jobs += [(("mix_out", t, i), "dve") for i in range(2)]
    jobs += [(("ffn_t", t, i), "act") for t in range(TILES) for i in range(2)]
    for hs in range(SIDES + 1):
        if hs < SIDES:
            jobs += [(("query", hs, 0), "act"), (("query", hs, 1), "act")]
        if hs:
            jobs += [(("scores", hs - 1), "dve")]
    return jobs


JOBS = psum_jobs()
JOB = {name: n for n, (name, _) in enumerate(JOBS)}
EMPTIED = {}
_seen = {"dve": 0, "act": 0}
for _name, _by in JOBS:
    _seen[_by] += 1
    EMPTIED[_name] = _seen[_by]
BANKS = 7


def build(nc, x_prompt, x_sample, state_ret, conv_state, weights, keys, params, consts, gain_ffn, gain_final,
          peer_down, peer_up, y_prompt, y_sample, ret_prompt, ret_sample, conv_prompt, conv_sample):
    ctx = ExitStack()
    with ctx:
        def sb(name, shape, dt=FP32):
            return ctx.enter_context(nc.sbuf_tensor(name, shape, dt))

        def sem(name):
            return ctx.enter_context(nc.semaphore(name))

        arena = sb("arena", [P, (DSLOTS + USLOTS) * D])
        w_ring = arena[:, 0:WSLOTS * KD * SEC].rearrange("p (s k n) -> p s k n", s=WSLOTS, k=KD)
        z_at = WSLOTS * KD * SEC
        z = arena[:, z_at:z_at + TILES * 4 * SEC].rearrange("p (t s n) -> p t s n", t=TILES, s=4)
        key_at = z_at + TILES * 4 * SEC
        keysT = arena[:, key_at:key_at + SIDES * KEYS].rearrange("p (s n) -> p s n", s=SIDES)
        queryT = arena[:, z_at:z_at + 4 * T].rearrange("p (b t) -> p b t", b=4)
        down_ring = arena[:, 0:DSLOTS * D].rearrange("p (s d) -> p s d", s=DSLOTS)
        up_ring = arena[:, DSLOTS * D:(DSLOTS + USLOTS) * D].rearrange("p (s d) -> p s d", s=USLOTS)

        xs = sb("xs", [P, TILES, D])
        hn = sb("hn", [P, TILES, D])
        scratch = hn[:, :, :].rearrange("p t d -> p (t d)")

        def scratch4(n):
            return scratch[:, n * RW:(n + 1) * RW].rearrange("p (h d) -> p h d", h=HEADS)
        q_rot, k_rot, k_dec, qT, qT_cross, kT, sc_dec, o_norm = (scratch4(n) for n in range(8))
        gate_tanh = scratch[:, 8 * RW:10 * RW].rearrange("p (b n) -> p b n", b=2)
        hT = sb("hT", [P, KD, T])
        loop_mem = hT[:, :, :].rearrange("p k t -> p (k t)")
        diag = loop_mem[:, 0:TOPK * P].rearrange("p (k n) -> p k n", k=TOPK)
        row_now = loop_mem[:, TOPK * P:TOPK * P + D]
        at = TOPK * P + D
        sc_now = loop_mem[:, at:at + 2 * KEYS].rearrange("p (s n) -> p s n", s=2)
        at += 2 * KEYS
        cand = loop_mem[:, at:at + TOPK * TOPK]
        cand_cut = loop_mem[:, at + TOPK * TOPK:at + 2 * TOPK * TOPK]
        at += 2 * TOPK * TOPK
        picks = loop_mem[:, at:at + 2 * TOPK * TOPK].rearrange("p (s a b) -> p s a b", s=2, a=TOPK)
        region_b = sb("region_b", [P, KD * T + CT * (SEQ + PAD + DEC + PAD) + CT * T])
        yT = region_b[:, 0:KD * T].rearrange("p (k t) -> p k t", k=KD)
        at = KD * T
        u_p = region_b[:, at:at + CT * (SEQ + PAD)].rearrange("p (c t) -> p c t", c=CT)
        row_gain = region_b[:, at:at + D]
        at += CT * (SEQ + PAD)
        u_s = region_b[:, at:at + CT * (DEC + PAD)].rearrange("p (c t) -> p c t", c=CT)
        at += CT * (DEC + PAD)
        conv = region_b[:, at:at + CT * T].rearrange("p (c t) -> p c t", c=CT)
        scores = region_b[:, 0:VT * 2 * KEYS].rearrange("p (v s n) -> p v s n", v=VT, s=2)

        cst = sb("cst", [P, C_WIDTH])
        par = sb("par", [P, G_WIDTH])
        half_ln = sb("half_ln", [P, 2 * CT])
        state = sb("state", [P, 2, HEADS, HD])
        ones_cw = sb("ones_cw", [P, P])
        neg_half = sb("neg_half", [P, 1])
        sq_sum = sb("sq_sum", [P, 3 * TILES])
        rstd = sb("rstd", [P, 3 * TILES])
        bn = sb("bn", [P, HEADS, 6])
        mv = sb("mv", [P, HEADS, 2])
        ret_rstd = sb("ret_rstd", [P, HEADS])
        var = sb("var", [P, T])
        rot_tmp = sb("rot_tmp", [P, HEADS, HD // 2])

        trig = cst[:, C_TRIG:C_DECAY].rearrange("p (t c n) -> p t c n", t=TILES, c=2)
        decay = cst[:, C_DECAY:C_CROSS].rearrange("p (h n) -> p h n", h=HEADS)
        cross = cst[:, C_CROSS:C_KDEC].rearrange("p (h n) -> p h n", h=HEADS)
        key_decay = cst[:, C_KDEC:C_IDENT].rearrange("p (c h) -> p c h", c=2)
        ident = cst[:, C_IDENT:C_FOLD]
        fold = cst[:, C_FOLD:C_IOTA]
        iota = cst[:, C_IOTA:C_WIDTH]

        sc_cut = var[:, 0:2 * KEYS].rearrange("p (s n) -> p s n", s=2)
        top_s = sb("top_s", [P, 2, TOPK])
        top_i = sb("top_i", [P, 2, TOPK], U32)
        top_f = sb("top_f", [P, 2, TOPK])
        best_s = sb("best_s", [P, TOPK])
        best_i = sb("best_i", [P, TOPK], U32)
        pair_i = sb("pair_i", [P, 2, TOPK], U32)
        pair_f = sb("pair_f", [P, 2, TOPK])
        picked = sb("picked", [P, 2, TOPK])
        expert_f = sb("expert_f", [P, TOPK])
        expert = sb("expert", [P, 2, TOPK], U32)
        neg_max = sb("neg_max", [P, 2])
        best_kept = sb("best_kept", [P, 2, TOPK])
        gate = sb("gate", [P, 2, TOPK])
        gate_sum = sb("gate_sum", [P, 2])
        dots = sb("dots", [P, TOPK])
        gl = sb("gl", [P, 2, TOPK])
        gl_tanh = sb("gl_tanh", [P, TOPK])
        weight = sb("weight", [P, TOPK])

        ps = ctx.enter_context(nc.psum_tensor("ps", [P, 8, SEC], FP32))
        product = ps[:, 4:6, :].rearrange("p b n -> p (b n)")
        sample_scores = ps[:, 7, :].rearrange("p (v s n) -> p v s n", v=2, s=2)

        def bank(name):
            return ps[:, JOB[name] % BANKS, :]

        s_x = sem("s_x")
        s_cst = sem("s_cst")
        s_par = sem("s_par")
        s_w = [sem(f"s_w{i}") for i in range(WSLOTS)]
        s_keys = sem("s_keys")
        s_gain = sem("s_gain")
        s_gain2 = sem("s_gain2")
        s_st = sem("s_st")
        s_pe = sem("s_pe")
        s_by = {"dve": sem("s_by_dve"), "act": sem("s_by_act")}
        s_setup = sem("s_setup")
        s_sq = sem("s_sq")
        s_rstd = sem("s_rstd")
        s_hn = sem("s_hn")
        s_wsec = sem("s_wsec")
        s_u = sem("s_u")
        s_conv = sem("s_conv")
        s_convout = sem("s_convout")
        s_gt = sem("s_gt")
        s_gate = sem("s_gate")
        s_csq = sem("s_csq")
        s_vr = sem("s_vr")
        s_yh = sem("s_yh")
        s_yt = sem("s_yt")
        s_yconv = sem("s_yconv")
        s_rot = sem("s_rot")
        s_ostat = sem("s_ostat")
        s_orstd = sem("s_orstd")
        s_on = sem("s_on")
        s_rep = sem("s_rep")
        s_ss = sem("s_ss")
        s_scores = sem("s_scores")
        s_out = sem("s_out")
        s_idx = sem("s_idx")
        s_exp = sem("s_exp")
        s_dn = [sem(f"s_dn{i}") for i in range(DSLOTS)]
        s_up = [sem(f"s_up{i}") for i in range(USLOTS)]
        s_dused = sem("s_dused")
        s_uused = sem("s_uused")
        s_poly = sem("s_poly")
        s_tanh = sem("s_tanh")
        s_wt = sem("s_wt")
        s_diag = sem("s_diag")
        s_acc = sem("s_acc")
        s_yout = sem("s_yout")

        def sections_used(s):
            return WEIGHT_ORDER.index(s) + 1

        block = ctx.enter_context(nc.Block())

        @block.sync
        def _(sp):
            sp.dma_start(xs[:, 0:SAMPLE, :], x_prompt.rearrange("(t p) d -> p t d", p=P)).then_inc(s_x, 16)
            sp.dma_start(xs[0:DEC, SAMPLE, :], x_sample).then_inc(s_x, 16)
            sp.dma_start(par[:, :], params).then_inc(s_par, 16)
            sp.dma_start(cst[:, :], consts).then_inc(s_cst, 16)
            for n, s in enumerate(WEIGHT_ORDER):
                if n >= WSLOTS:
                    sp.wait_ge(s_wsec, n - WSLOTS + 1)
                sp.dma_start(w_ring[:, n % WSLOTS], weights[s]).then_inc(s_w[n % WSLOTS], 16)
                if n == 0:
                    sp.dma_start(u_s[:, :, 0:PAD], conv_state).then_inc(s_st, 16)
                    sp.dma_start(state[:, 1], state_ret).then_inc(s_st, 16)
                    sp.dma_start(keysT, keys).then_inc(s_keys, 16)
                if WEIGHT_ORDER[n] == S_OUT + 1:
                    sp.wait_ge(s_u, 1)
                    sp.dma_start(conv_prompt, u_p[:, :, SEQ:SEQ + PAD]).then_inc(s_convout, 16)
                    sp.dma_start(conv_sample, u_s[:, :, DEC:DEC + PAD]).then_inc(s_convout, 16)
                    sp.wait_ge(s_convout, 32)
                    sp.wait_ge(s_conv, 1)
                    sp.dma_start(row_gain, gain_ffn.to_broadcast([P, D])).then_inc(s_gain, 16)
            sp.wait_ge(s_by["dve"], EMPTIED[("ret_state", SAMPLE)])
            sp.dma_start(ret_prompt, state[:, 0]).then_inc(s_out, 16)
            sp.dma_start(ret_sample, state[:, 1]).then_inc(s_out, 16)
            sp.wait_ge(s_hn, 2 * TILES)
            for j in range(1, FOLDED):
                sp.dma_start(hn[j * DEC:(j + 1) * DEC, SAMPLE, :], hn[0:DEC, SAMPLE, :]).then_inc(s_rep, 16)
            sp.wait_ge(s_idx, VT)
            sp.dma_start(row_gain, gain_final.to_broadcast([P, D])).then_inc(s_gain2, 16)
            for t in range(TILES):
                sp.wait_ge(s_yout, t + 1)
                out = y_prompt[t * P:(t + 1) * P, :] if t < SAMPLE else y_sample
                sp.dma_start(out, xs[0:ROWS[t], t, :]).then_inc(s_out, 16)
            sp.wait_ge(s_out, 16 * (2 + TILES))
            sp.wait_ge(s_convout, 32)

        @block.gpsimd
        def _(pool):
            nc.gpsimd.memset(neg_half[:, :], -0.5)
            pool.drain()

            def inverse_root(out, in_, rows, n, ready):
                nc.gpsimd.tensor_scalar(out=out, in0=in_, scalar1=1.0 / n, scalar2=EPS, op0=ALU.mult, op1=ALU.add)
                pool.drain()
                width = out.shape[-1]
                power = neg_half[0:rows, 0:1]
                nc.gpsimd.tensor_tensor(out=out, in0=out, in1=power if width == 1 else power.to_broadcast([rows, width]),
                                        op=ALU.pow).then_inc(ready, 1)

            for t in range(TILES):
                pool.wait_ge(s_sq, t + 1)
                inverse_root(rstd[0:ROWS[t], t:t + 1], sq_sum[0:ROWS[t], t:t + 1], ROWS[t], D, s_rstd)

            half = HD // 2
            pool.wait_ge(s_cst, 16)
            for t in range(TILES):
                r = ROWS[t]
                pool.wait_ge(s_by["act"], EMPTIED[("qkvg", S_K, t)])
                if t:
                    pool.wait_ge(s_pe, JOB[("ret_state", t - 1)] + 1)
                cos = trig[0:r, t, 0].unsqueeze(1).to_broadcast([r, HEADS, half])
                sin = trig[0:r, t, 1].unsqueeze(1).to_broadcast([r, HEADS, half])
                tmp = rot_tmp[0:r]
                for col, dst in ((0, q_rot), (1, k_rot)):
                    src = z[0:r, t, col].rearrange("p (h d) -> p h d", h=HEADS)
                    x1, x2 = src[:, :, 0:half], src[:, :, half:HD]
                    for a, b, o, op in ((x1, x2, dst[0:r, :, 0:half], ALU.subtract),
                                        (x2, x1, dst[0:r, :, half:HD], ALU.add)):
                        nc.gpsimd.tensor_tensor(out=o, in0=a, in1=cos, op=ALU.mult)
                        nc.gpsimd.tensor_tensor(out=tmp, in0=b, in1=sin, op=ALU.mult)
                        pool.drain()
                        nc.gpsimd.tensor_tensor(out=o, in0=o, in1=tmp, op=op)
                        pool.drain()
                kd = key_decay[0:r, 1 if t == SAMPLE else 0].unsqueeze(2).to_broadcast([r, HEADS, HD])
                nc.gpsimd.tensor_tensor(out=k_dec[0:r], in0=k_rot[0:r], in1=kd, op=ALU.mult).then_inc(s_rot, 1)
                if t == 0:
                    pool.wait_ge(s_by["dve"], EMPTIED[("ln_var", 1)])
                    inverse_root(var[:, :], var[:, :], P, 1, s_vr)
                pool.wait_ge(s_ostat, t + 1)
                inverse_root(ret_rstd[0:r, :], mv[0:r, :, 1], r, 1, s_orstd)
            for t in range(TILES):
                pool.wait_ge(s_sq, TILES + t + 1)
                c = TILES + t
                inverse_root(rstd[0:ROWS[t], c:c + 1], sq_sum[0:ROWS[t], c:c + 1], ROWS[t], D, s_rstd)

            def gathers(vt, u, first):
                pool.wait_ge(s_idx, vt + 1)
                pool.nop(nofuse=True)
                for k in range(TOPK):
                    if not first or k >= DSLOTS:
                        pool.wait_ge(s_dused, vt * TOPK + (k - DSLOTS + 1))
                        pool.nop(nofuse=True)
                    pool.indirect_dma_start(down_ring[:, k % DSLOTS, :], None, peer_down,
                                            bass.IndirectOffsetOnAxis(ap=expert[:, u, k:k + 1], axis=0))\
                        .then_inc(s_dn[k % DSLOTS], 16)
                for k in range(TOPK):
                    if not first:
                        pool.wait_ge(s_uused, vt * TOPK + (k - USLOTS + 1))
                        pool.nop(nofuse=True)
                    pool.indirect_dma_start(up_ring[:, k, :], None, peer_up,
                                            bass.IndirectOffsetOnAxis(ap=expert[:, u, k:k + 1], axis=0))\
                        .then_inc(s_up[k], 16)

            pool.wait_ge(s_scores, 1)
            gathers(0, 0, True)
            gathers(1, 1, False)
            with pool.Fori(1, VT // 2) as pair:
                for u in range(2):
                    gathers(pair * 2 + u, u, False)
            for t in range(TILES):
                pool.wait_ge(s_sq, 2 * TILES + t + 1)
                c = 2 * TILES + t
                inverse_root(rstd[0:ROWS[t], c:c + 1], sq_sum[0:ROWS[t], c:c + 1], ROWS[t], D, s_rstd)

        @block.scalar
        def _(act):
            def square_sum(src, col, rows, junk):
                nc.scalar.activation(junk, src, ACT.Square, accum_out=sq_sum[0:rows, col:col + 1]).then_inc(s_sq, 1)

            def emptied(ins):
                ins.then_inc(s_by["act"], 1)

            def filled(name):
                act.wait_ge(s_pe, JOB[name] + 1)

            act.wait_ge(s_x, 32)
            for t in range(TILES):
                square_sum(xs[0:ROWS[t], t], t, ROWS[t], hn[0:ROWS[t], t])
            for s in (S_A, S_B):
                func, scale = (ACT.Copy, 0.5) if s == S_A else (ACT.Tanh, 0.5)
                for c in range(CT + 1):
                    filled(("glu", s, c))
                    src = bank(("glu", s, c))
                    if c < CT:
                        dst = u_p[:, c, PAD:PAD + SEQ] if s == S_A else conv[:, c, 0:SEQ]
                    else:
                        src = src[:, 0:CT * DEC].rearrange("p (c t) -> p c t", c=CT)
                        dst = u_s[:, :, PAD:PAD + DEC] if s == S_A else conv[:, :, SEQ:T]
                    emptied(nc.scalar.activation(dst, src, func, scale=scale))
            for s in (S_Q, S_K, S_V, S_G):
                for t in range(TILES):
                    r = ROWS[t]
                    filled(("qkvg", s, t))
                    src = bank(("qkvg", s, t))[0:r]
                    if s == S_G:
                        if t >= 2:
                            act.wait_ge(s_gate, t - 1)
                        nc.scalar.activation(gate_tanh[0:r, t % 2], src, ACT.Tanh, scale=0.5)
                        ins = nc.scalar.activation(z[0:r, t, s], src, ACT.Copy, scale=0.5)
                        emptied(ins)
                    else:
                        emptied(nc.scalar.activation(z[0:r, t, s], src, ACT.Copy))
            act.wait_ge(s_by["dve"], EMPTIED[("ln_mean", 1)])
            for c in range(CT):
                nc.scalar.activation(yT[:, HEADS + c, :], conv[:, c, :], ACT.Square).then_inc(s_csq, 1)
            act.wait_ge(s_yh, 1)
            for c in range(CT):
                nc.scalar.activation(yT[:, HEADS + c, :], conv[:, c, :], ACT.Tanh).then_inc(s_yt, 1)
            for t in range(TILES):
                act.wait_ge(s_by["dve"], EMPTIED[("mix_out", t, 1)])
                square_sum(xs[0:ROWS[t], t], TILES + t, ROWS[t], hn[0:ROWS[t], t])
            for t in range(TILES):
                for i in range(2):
                    name = ("ffn_t", t, i)
                    filled(name)
                    r = ROWS[t]
                    src = bank(name).rearrange("p (k t) -> p k t", k=4)[:, :, 0:r]
                    emptied(nc.scalar.activation(hT[:, 4 * i:4 * i + 4, t * P:t * P + r], src, ACT.Copy))
            for hs in range(SIDES):
                for i in range(2):
                    name = ("query", hs, i)
                    filled(name)
                    if i == 0 and hs >= 4:
                        act.wait_ge(s_pe, JOB[("scores", hs - 4)] + 1)
                    lo, hi = (0, SEQ) if i == 0 else (SEQ, T)
                    emptied(nc.scalar.activation(queryT[:, hs % 4, lo:hi], bank(name)[:, 0:hi - lo], ACT.Copy))

            def softmax_exp(vt, u):
                act.wait_ge(s_idx, vt + 1)
                nc.scalar.activation(gate[:, u, :], best_kept[:, u, :], ACT.Exp, bias=neg_max[:, u:u + 1],
                                     accum_out=gate_sum[:, u:u + 1]).then_inc(s_exp, 1)

            def head_tile(vt, u, base, last):
                act.wait_ge(s_poly, vt + 1)
                nc.scalar.activation(gl_tanh[:, :], gl[:, 0, :], ACT.Tanh, scale=math.sqrt(2.0 / math.pi))\
                    .then_inc(s_tanh, 1)
                act.wait_ge(s_wt, vt + 1)
                for k in range(TOPK):
                    nc.scalar.activation(diag[:, k, :], base, ACT.Copy, scale=weight[:, k:k + 1]).then_inc(s_diag, 1)
                if not last:
                    softmax_exp(vt + 1, 1 - u)

            softmax_exp(0, 0)
            head_tile(0, 0, ident, False)
            act.wait_ge(s_uused, TOPK)
            head_tile(1, 1, ident, False)
            with act.Fori(1, (VT - 2) // 2) as pair:
                for u in range(2):
                    act.wait_ge(s_uused, (pair * 2 + u) * TOPK)
                    act.nop(nofuse=True)
                    head_tile(pair * 2 + u, u, ident, False)
            for u in range(2):
                act.wait_ge(s_uused, (VT - 2 + u) * TOPK)
                head_tile(VT - 2 + u, u, fold, u == 1)
            act.wait_ge(s_acc, VT)
            for t in range(TILES):
                square_sum(xs[0:ROWS[t], t], 2 * TILES + t, ROWS[t], hn[0:ROWS[t], t])

        @block.vector
        def _(dve):
            v = nc.vector

            def emptied(ins):
                ins.then_inc(s_by["dve"], 1)

            def filled(name):
                dve.wait_ge(s_pe, JOB[name] + 1)

            v.memset(ones_cw[:, :], 1.0 / CW)
            v.memset(u_p[:, :, 0:PAD], 0.0).then_inc(s_setup, 1)
            dve.wait_ge(s_par, 16)
            v.tensor_scalar(out=half_ln[:, :], in0=par[:, G_LNG:G_TAPS], scalar1=0.5, scalar2=None, op0=ALU.mult)
            for t in range(TILES):
                r = ROWS[t]
                dve.wait_ge(s_rstd, t + 1)
                v.tensor_scalar(out=hn[0:r, t], in0=xs[0:r, t], scalar1=rstd[0:r, t:t + 1], scalar2=None,
                                op0=ALU.mult).then_inc(s_hn, 1)
            for t in range(TILES):
                r = ROWS[t]
                for i in range(2):
                    name = ("norm_t", t, i)
                    filled(name)
                    src = bank(name).rearrange("p (k t) -> p k t", k=4)[:, :, 0:r]
                    gain = par[:, G_MIX + 4 * i:G_MIX + 4 * i + 4].unsqueeze(2).to_broadcast([P, 4, r])
                    emptied(v.tensor_tensor(out=hT[:, 4 * i:4 * i + 4, t * P:t * P + r], in0=src, in1=gain,
                                            op=ALU.mult))
            dve.wait_ge(s_by["act"], EMPTIED[("glu", S_B, CT)])
            dve.wait_ge(s_st, 32)
            for c in range(CT):
                v.scalar_tensor_tensor(out=u_p[:, c, PAD:PAD + SEQ], in0=conv[:, c, 0:SEQ], scalar=1.0,
                                       in1=u_p[:, c, PAD:PAD + SEQ], op0=ALU.add, op1=ALU.mult)
            v.scalar_tensor_tensor(out=u_s[:, :, PAD:PAD + DEC], in0=conv[:, :, SEQ:T], scalar=1.0,
                                   in1=u_s[:, :, PAD:PAD + DEC], op0=ALU.add, op1=ALU.mult).then_inc(s_u, 1)
            dve.drain()
            for j in range(TAPS):
                for c in range(CT):
                    tap = par[:, G_TAPS + c * TAPS + j:G_TAPS + c * TAPS + j + 1]
                    for src, lo, n in ((u_p, 0, SEQ), (u_s, SEQ, DEC)):
                        out = conv[:, c, lo:lo + n]
                        if j == 0:
                            v.tensor_scalar(out=out, in0=src[:, c, 0:n], scalar1=tap,
                                            scalar2=par[:, G_BIAS + c:G_BIAS + c + 1], op0=ALU.mult, op1=ALU.add)
                        else:
                            last = v.scalar_tensor_tensor(out=out, in0=src[:, c, j:j + n], scalar=tap, in1=out,
                                                          op0=ALU.mult, op1=ALU.add)
                if j < TAPS - 1:
                    dve.drain()
            last.then_inc(s_conv, 1)
            for t in range(TILES):
                r = ROWS[t]
                dve.wait_ge(s_by["act"], EMPTIED[("qkvg", S_G, t)])
                v.scalar_tensor_tensor(out=z[0:r, t, S_G], in0=gate_tanh[0:r, t % 2], scalar=1.0, in1=z[0:r, t, S_G],
                                       op0=ALU.add, op1=ALU.mult).then_inc(s_gate, 1)
            for i, (lo, hi) in enumerate(((0, SEQ), (SEQ, T))):
                filled(("ln_mean", i))
                mean = bank(("ln_mean", i))[:, 0:hi - lo].unsqueeze(1).to_broadcast([P, CT, hi - lo])
                emptied(v.tensor_tensor(out=conv[:, :, lo:hi], in0=conv[:, :, lo:hi], in1=mean, op=ALU.subtract))
            for i, (lo, hi) in enumerate(((0, SEQ), (SEQ, T))):
                filled(("ln_var", i))
                emptied(v.tensor_copy(var[:, lo:hi], bank(("ln_var", i))[:, 0:hi - lo]))
            dve.wait_ge(s_vr, 1)
            v.tensor_tensor(out=conv[:, :, :], in0=conv[:, :, :], in1=var[:, :].unsqueeze(1).to_broadcast([P, CT, T]),
                            op=ALU.mult)
            dve.drain()
            for c in range(CT):
                last = v.tensor_scalar(out=conv[:, c, :], in0=conv[:, c, :], scalar1=half_ln[:, c:c + 1],
                                       scalar2=half_ln[:, CT + c:CT + c + 1], op0=ALU.mult, op1=ALU.add)
            last.then_inc(s_yh, 1)
            dve.wait_ge(s_yt, CT)
            v.scalar_tensor_tensor(out=yT[:, HEADS:KD, :], in0=yT[:, HEADS:KD, :], scalar=1.0, in1=conv[:, :, :],
                                   op0=ALU.add, op1=ALU.mult).then_inc(s_yconv, 1)
            for t in range(TILES):
                r = ROWS[t]
                which, length = (1, DEC) if t == SAMPLE else (0, P)

                def four(name, n=r):
                    return bank(name).rearrange("p (h n) -> p h n", h=HEADS)[:, :, 0:n]
                name = ("ret_qT", t)
                filled(name)
                v.tensor_copy(qT[:, :, 0:r], four(name))
                emptied(v.tensor_tensor(out=qT_cross[:, :, 0:r], in0=four(name), in1=cross[:, :, 0:r], op=ALU.mult))
                name = ("ret_kT", t)
                filled(name)
                emptied(v.tensor_copy(kT[:, :, 0:r], four(name)))
                name = ("ret_scores", t)
                filled(name)
                emptied(v.tensor_tensor(out=sc_dec[0:r, :, 0:r], in0=four(name)[0:r], in1=decay[0:r, :, 0:r],
                                        op=ALU.mult))
                name = ("ret_out", t)
                filled(name)
                o = bank(name)[0:r].rearrange("p (h d) -> p h d", h=HEADS)
                for h in range(HEADS):
                    v.bn_stats(bn[0:r, h, :], o[:, h, :])
                dve.drain()
                for h in range(HEADS):
                    last = v.bn_aggr(mv[0:r, h, :], bn[0:r, h, :])
                last.then_inc(s_ostat, 1)
                dve.wait_ge(s_orstd, t + 1)
                for h in range(HEADS):
                    last = v.tensor_scalar(out=o_norm[0:r, h, :], in0=o[:, h, :], scalar1=mv[0:r, h, 0:1],
                                           scalar2=ret_rstd[0:r, h:h + 1], op0=ALU.subtract, op1=ALU.mult)
                emptied(last)
                dve.drain()
                v.tensor_tensor(out=o_norm[0:r], in0=o_norm[0:r], in1=z[0:r, t, S_G].rearrange("p (h d) -> p h d", h=HEADS),
                                op=ALU.mult).then_inc(s_on, 1)
                name = ("ret_state", t)
                filled(name)
                add = bank(name).rearrange("p (h d) -> p h d", h=HEADS)
                if t == 0:
                    last = v.tensor_copy(state[:, 0], add)
                else:
                    for h, g in enumerate(gammas(length)):
                        last = v.scalar_tensor_tensor(out=state[:, which, h], in0=state[:, which, h], scalar=g,
                                                      in1=add[:, h], op0=ALU.mult, op1=ALU.add)
                emptied(last)
                name = ("ret_yT", t)
                filled(name)
                gain = par[:, G_RET:G_RET + HEADS].unsqueeze(2).to_broadcast([P, HEADS, r])
                emptied(v.tensor_tensor(out=yT[:, 0:HEADS, t * P:t * P + r], in0=four(name), in1=gain, op=ALU.mult))
            for t in range(TILES):
                for i in range(2):
                    name = ("mix_out", t, i)
                    filled(name)
                    part = xs[0:ROWS[t], t, i * SEC:(i + 1) * SEC]
                    emptied(v.tensor_tensor(out=part, in0=bank(name)[0:ROWS[t]], in1=part, op=ALU.add))
            dve.wait_ge(s_gain, 16)
            for t in range(TILES):
                r = ROWS[t]
                dve.wait_ge(s_rstd, TILES + t + 1)
                v.scalar_tensor_tensor(out=hn[0:r, t], in0=xs[0:r, t], scalar=rstd[0:r, TILES + t:TILES + t + 1],
                                       in1=row_gain[0:r, :], op0=ALU.mult, op1=ALU.mult).then_inc(s_hn, 1)
            dve.wait_ge(s_convout, 32)
            by_head = scores[:, 0:SAMPLE * PH].rearrange("p (t h) s n -> p t h s n", t=SAMPLE)
            for hs in range(SIDES):
                name = ("scores", hs)
                filled(name)
                src = bank(name).rearrange("p (t n) -> p t n", t=SAMPLE)
                emptied(v.tensor_copy(by_head[:, :, hs // 2, hs % 2, :], src))
            v.tensor_copy(scores[:, SAMPLE * PH:VT], sample_scores).then_inc(s_scores, 1)
            dve.drain()

            def top16(values, cut, best, index):
                v.max(best[:, 0:8], values)
                dve.drain()
                v.max_index(index[:, 0:8], best[:, 0:8], values)
                v.match_replace(cut, best[:, 0:8], values, LOWEST)
                dve.drain()
                v.max(best[:, 8:16], cut)
                dve.drain()
                v.max_index(index[:, 8:16], best[:, 8:16], cut)

            def choose(vt, u):
                at = bass.ds(vt * 2 * KEYS, 2 * KEYS)
                v.tensor_copy(sc_now.rearrange("p s n -> p (s n)"), region_b[:, at])
                dve.drain()
                for s in range(2):
                    top16(sc_now[:, s, :], sc_cut[:, s, :], top_s[:, s, :], top_i[:, s, :])
                dve.drain()
                v.tensor_copy(top_f[:, :, :], top_i[:, :, :])
                v.tensor_tensor(out=cand[:, :].rearrange("p (a b) -> p a b", a=TOPK),
                                in0=top_s[:, 0, :].unsqueeze(2).to_broadcast([P, TOPK, TOPK]),
                                in1=top_s[:, 1, :].unsqueeze(1).to_broadcast([P, TOPK, TOPK]), op=ALU.add)
                dve.drain()
                top16(cand[:, :], cand_cut[:, :], best_s[:, :], best_i[:, :])
                dve.drain()
                v.tensor_copy(best_kept[:, u, :], best_s[:, :])
                v.tensor_scalar(out=neg_max[:, u:u + 1], in0=best_s[:, 0:1], scalar1=-1.0, scalar2=None, op0=ALU.mult)
                v.tensor_scalar(out=pair_i[:, 0, :], in0=best_i[:, :], scalar1=4, scalar2=None,
                                op0=ALU.logical_shift_right)
                v.tensor_scalar(out=pair_i[:, 1, :], in0=best_i[:, :], scalar1=TOPK - 1, scalar2=None,
                                op0=ALU.bitwise_and)
                dve.drain()
                v.tensor_copy(pair_f[:, :, :], pair_i[:, :, :])
                dve.drain()
                for s in range(2):
                    v.tensor_tensor(out=picks[:, s], in0=pair_f[:, s, :].unsqueeze(2).to_broadcast([P, TOPK, TOPK]),
                                    in1=iota.unsqueeze(1).to_broadcast([P, TOPK, TOPK]), op=ALU.is_equal)
                dve.drain()
                for s in range(2):
                    v.tensor_tensor(out=picks[:, s], in0=picks[:, s],
                                    in1=top_f[:, s, :].unsqueeze(1).to_broadcast([P, TOPK, TOPK]), op=ALU.mult)
                dve.drain()
                v.tensor_reduce(out=picked[:, :, :], in_=picks[:, :, :, :], axis=AX.X, op=ALU.add)
                dve.drain()
                v.scalar_tensor_tensor(out=expert_f[:, :], in0=picked[:, 0, :], scalar=float(KEYS), in1=picked[:, 1, :],
                                       op0=ALU.mult, op1=ALU.add)
                dve.drain()
                v.tensor_copy(expert[:, u, :], expert_f[:, :]).then_inc(s_idx, 1)

            def weigh(vt, u, tile):
                v.tensor_copy(row_now, hn[:, :, :].rearrange("p t d -> p (t d)")[:, bass.ds(tile * D, D)])
                dve.drain()
                for k in range(TOPK):
                    dve.wait_ge(s_dn[k % DSLOTS], vt * 32 + 16 * (k // DSLOTS + 1))
                    v.tensor_tensor_reduce(out=product, in0=down_ring[:, k % DSLOTS, :], in1=row_now, scale=1.0,
                                           scalar=0.0, op0=ALU.mult, op1=ALU.add, accum_out=dots[:, k:k + 1])\
                        .then_inc(s_dused, 1)
                    dve.drain()
                v.tensor_tensor(out=gl[:, 1, :], in0=dots[:, :], in1=dots[:, :], op=ALU.mult)
                dve.drain()
                v.tensor_scalar(out=gl[:, 1, :], in0=gl[:, 1, :], scalar1=0.044715, scalar2=1.0, op0=ALU.mult,
                                op1=ALU.add)
                dve.drain()
                v.tensor_tensor(out=gl[:, 0, :], in0=gl[:, 1, :], in1=dots[:, :], op=ALU.mult).then_inc(s_poly, 1)
                dve.wait_ge(s_exp, vt + 1)
                dve.nop(nofuse=True)
                v.reciprocal(gate_sum[:, u:u + 1], gate_sum[:, u:u + 1])
                dve.drain()
                v.scalar_tensor_tensor(out=dots[:, :], in0=gate[:, u, :], scalar=gate_sum[:, u:u + 1], in1=dots[:, :],
                                       op0=ALU.mult, op1=ALU.mult)
                dve.drain()
                v.tensor_scalar(out=dots[:, :], in0=dots[:, :], scalar1=0.5, scalar2=None, op0=ALU.mult)
                dve.drain()
                dve.wait_ge(s_tanh, vt + 1)
                dve.nop(nofuse=True)
                v.scalar_tensor_tensor(out=weight[:, :], in0=gl_tanh[:, :], scalar=1.0, in1=dots[:, :],
                                       op0=ALU.add, op1=ALU.mult).then_inc(s_wt, 1)

            def add(vt, u, tile, rows):
                dve.wait_ge(s_uused, (vt + 1) * TOPK)
                dve.nop(nofuse=True)
                part = xs[:, :, :].rearrange("p t d -> p (t d)")[0:rows, bass.ds(tile * D, D)]
                v.tensor_tensor(out=part, in0=ps[0:rows, 2 * u:2 * u + 2, :].rearrange("p b n -> p (b n)"), in1=part,
                                op=ALU.add).then_inc(s_acc, 1)

            choose(0, 0)
            weigh(0, 0, 0)
            choose(1, 1)
            weigh(1, 1, 0)
            add(0, 0, 0, P)
            choose(2, 0)
            with dve.Fori(1, (VT - 2) // 2) as pair:
                for u in range(2):
                    vt = pair * 2 + u
                    weigh(vt, u, vt >> 3)
                    add(vt - 1, 1 - u, (vt - 1) >> 3, P)
                    choose(vt + 1, 1 - u)
            dve.wait_ge(s_rep, 16 * (FOLDED - 1))
            weigh(VT - 2, 0, SAMPLE)
            add(VT - 3, 1, SAMPLE - 1, P)
            choose(VT - 1, 1)
            weigh(VT - 1, 1, SAMPLE)
            add(VT - 2, 0, SAMPLE, DEC)
            dve.drain()
            add(VT - 1, 1, SAMPLE, DEC)
            dve.drain()
            dve.wait_ge(s_gain2, 16)
            for t in range(TILES):
                r = ROWS[t]
                dve.wait_ge(s_rstd, 2 * TILES + t + 1)
                v.scalar_tensor_tensor(out=xs[0:r, t], in0=xs[0:r, t], scalar=rstd[0:r, 2 * TILES + t:2 * TILES + t + 1],
                                       in1=row_gain[0:r, :], op0=ALU.mult, op1=ALU.mult).then_inc(s_yout, 1)

        @block.tensor
        def _(pe):
            mm = nc.tensor.matmul

            def open_bank(name):
                n = JOB[name]
                if n >= BANKS:
                    before, by = JOBS[n - BANKS]
                    pe.wait_ge(s_by[by], EMPTIED[before])
                return bank(name)

            def done(ins):
                ins.then_inc(s_pe, 1)

            def section(s):
                n = WEIGHT_ORDER.index(s)
                pe.wait_ge(s_w[n % WSLOTS], 16 * (n // WSLOTS + 1))
                return w_ring[:, n % WSLOTS]

            pe.wait_ge(s_cst, 16)

            def transposes(name, sources, r):
                out = open_bank(name)
                for j, src in enumerate(sources):
                    last = nc.tensor.transpose(out[:, j * P:j * P + r], src, ident[0:r, 0:r])
                done(last)

            def row_transposes(kind, first):
                for t in range(TILES):
                    pe.wait_ge(s_hn, first + t + 1)
                    for i in range(2):
                        transposes((kind, t, i), [hn[0:ROWS[t], t, k * P:(k + 1) * P] for k in range(4 * i, 4 * i + 4)],
                                   ROWS[t])

            row_transposes("norm_t", 0)
            pe.wait_ge(s_by["dve"], EMPTIED[("norm_t", SAMPLE, 1)])
            for s in (S_A, S_B):
                w = section(s)
                for c in range(CT):
                    out = open_bank(("glu", s, c))
                    for k in range(KD):
                        last = mm(out, w[:, k, c * P:(c + 1) * P], hT[:, k, 0:SEQ], start=k == 0, stop=k == KD - 1)
                    done(last)
                out = open_bank(("glu", s, CT))
                for c in range(CT):
                    for k in range(KD):
                        last = mm(out[:, c * DEC:(c + 1) * DEC], w[:, k, c * P:(c + 1) * P], hT[:, k, SEQ:T],
                                  start=k == 0, stop=k == KD - 1)
                last.then_inc(s_pe, 1)
                pe.drain().then_inc(s_wsec, 1)

            def rows_times(name, lhs, w, r, lo):
                out = open_bank(name)
                for k in range(KD):
                    last = mm(out[0:r, :], lhs[:, k, lo:lo + r], w[:, k, :], start=k == 0, stop=k == KD - 1)
                done(last)

            for s in (S_Q, S_K, S_V, S_G):
                w = section(s)
                for t in range(TILES):
                    rows_times(("qkvg", s, t), hT, w, ROWS[t], t * P)
                pe.drain().then_inc(s_wsec, 1)
            pe.wait_ge(s_conv, 1)
            for i, (lo, hi) in enumerate(((0, SEQ), (SEQ, T))):
                out = open_bank(("ln_mean", i))
                for c in range(CT):
                    last = mm(out[:, 0:hi - lo], ones_cw[:, :], conv[:, c, lo:hi], start=c == 0, stop=c == CT - 1)
                done(last)
            pe.wait_ge(s_csq, CT)
            for i, (lo, hi) in enumerate(((0, SEQ), (SEQ, T))):
                out = open_bank(("ln_var", i))
                for c in range(CT):
                    last = mm(out[:, 0:hi - lo], ones_cw[:, :], yT[:, HEADS + c, lo:hi], start=c == 0,
                              stop=c == CT - 1)
                done(last)
            for t in range(TILES):
                r = ROWS[t]
                v_rows = z[0:r, t, S_V].rearrange("p (h d) -> p h d", h=HEADS)
                pe.wait_ge(s_rot, t + 1)
                transposes(("ret_qT", t), [q_rot[0:r, h, :] for h in range(HEADS)], r)
                transposes(("ret_kT", t), [k_rot[0:r, h, :] for h in range(HEADS)], r)
                pe.wait_ge(s_by["dve"], EMPTIED[("ret_kT", t)])
                out = open_bank(("ret_scores", t))
                for h in range(HEADS):
                    last = mm(out[0:r, h * P:h * P + r], kT[:, h, 0:r], qT[:, h, 0:r], start=True, stop=True)
                done(last)
                pe.wait_ge(s_by["dve"], EMPTIED[("ret_scores", t)])
                out = open_bank(("ret_out", t))
                for h in range(HEADS):
                    part = out[0:r, h * HD:(h + 1) * HD]
                    last = mm(part, sc_dec[0:r, h, 0:r], v_rows[:, h, :], start=True, stop=t == 0)
                    if t:
                        if h == 0 and t < SAMPLE:
                            pe.wait_ge(s_by["dve"], EMPTIED[("ret_state", t - 1)])
                        if h == 0 and t == SAMPLE:
                            pe.wait_ge(s_st, 32)
                        last = mm(part, qT_cross[:, h, 0:r], state[:, 1 if t == SAMPLE else 0, h, :], start=False,
                                  stop=True)
                done(last)
                out = open_bank(("ret_state", t))
                for h in range(HEADS):
                    last = mm(out[:, h * HD:(h + 1) * HD], k_dec[0:r, h, :], v_rows[:, h, :], start=True, stop=True)
                done(last)
                pe.wait_ge(s_on, t + 1)
                transposes(("ret_yT", t), [o_norm[0:r, h, :] for h in range(HEADS)], r)
            pe.wait_ge(s_yconv, 1)
            pe.wait_ge(s_by["dve"], EMPTIED[("ret_yT", SAMPLE)])
            w_out = [section(S_OUT), section(S_OUT + 1)]
            for t in range(TILES):
                for i in range(2):
                    rows_times(("mix_out", t, i), yT, w_out[i], ROWS[t], t * P)
            pe.drain().then_inc(s_wsec, 2)
            row_transposes("ffn_t", TILES)
            pe.wait_ge(s_by["act"], EMPTIED[("ffn_t", SAMPLE, 1)])
            pe.wait_ge(s_keys, 16)
            for hs in range(SIDES + 1):
                if hs < SIDES:
                    if hs % 4 == 0:
                        w = section(S_QUERY + hs // 4)
                    cols = slice((hs % 4) * P, (hs % 4 + 1) * P)
                    for i, (lo, hi) in enumerate(((0, SEQ), (SEQ, T))):
                        out = open_bank(("query", hs, i))
                        for k in range(KD):
                            last = mm(out[:, 0:hi - lo], w[:, k, cols], hT[:, k, lo:hi], start=k == 0,
                                      stop=k == KD - 1)
                        done(last)
                    if hs % 4 == 3:
                        pe.drain().then_inc(s_wsec, 1)
                if hs:
                    side = hs - 1
                    head = side // 2
                    pe.wait_ge(s_by["act"], EMPTIED[("query", side, 1)])
                    out = open_bank(("scores", side))
                    j = head % FOLDED
                    mm(ps[j * DEC:(j + 1) * DEC, 7, (head // FOLDED * 2 + side % 2) * KEYS:][:, 0:KEYS],
                       queryT[:, side % 4, SEQ:T], keysT[:, side, :], start=True, stop=True)
                    for t in range(SAMPLE):
                        last = mm(out[:, t * KEYS:(t + 1) * KEYS], queryT[:, side % 4, t * P:(t + 1) * P],
                                  keysT[:, side, :], start=True, stop=True)
                    done(last)

            def sum_up(vt, u, first):
                if not first:
                    pe.wait_ge(s_acc, vt - 1)
                    pe.nop(nofuse=True)
                for k in range(TOPK):
                    pe.wait_ge(s_up[k], vt * 16 + 16)
                    pe.wait_ge(s_diag, vt * TOPK + k + 1)
                    for half in range(2):
                        last = mm(ps[:, 2 * u + half, :], diag[:, k, :], up_ring[:, k, half * SEC:(half + 1) * SEC],
                                  start=k == 0, stop=k == TOPK - 1)
                    last.then_inc(s_uused, 1)

            sum_up(0, 0, True)
            sum_up(1, 1, True)
            with pe.Fori(1, VT // 2) as pair:
                for u in range(2):
                    sum_up(pair * 2 + u, u, False)


_INS = ["x_prompt", "x_sample", "state_ret", "conv_state", "weights", "keys", "params", "consts", "gain_ffn",
        "gain_final", "peer_down", "peer_up"]
_OUTS = [("y_prompt", (SEQ, D)), ("y_sample", (DEC, D)), ("ret_prompt", (P, HEADS, HD)), ("ret_sample", (P, HEADS, HD)),
         ("conv_prompt", (P, CT, PAD)), ("conv_sample", (P, CT, PAD))]


def lay_out(inputs):
    a = {k: np.asarray(v) for k, v in inputs.items()}
    w_all = np.concatenate([a["w_in"][0], a["w_out"][0], a["peer_query"][0]], axis=1)
    weights = w_all.reshape(KD, P, SECTIONS, SEC).transpose(2, 1, 0, 3)

    def columns(x):
        return x.reshape(-1, P).T
    taps = a["conv_dw"][0].reshape(TAPS, CT, P).transpose(2, 1, 0).reshape(P, CT * TAPS)
    params = np.concatenate([columns(a["norm_mix"][0]), columns(a["ret_gn_gain"][0]), columns(a["conv_dw_bias"][0]),
                             columns(a["conv_ln_gain"][0]), columns(a["conv_ln_bias"][0]), taps], axis=1)
    out = {
        "x_prompt": a["x_prompt"][0], "x_sample": a["x_sample"][0],
        "state_ret": a["state_retention"][0, 0].transpose(1, 0, 2),
        "conv_state": a["state_conv"][0, 0].reshape(PAD, CT, P).transpose(2, 1, 0),
        "weights": weights,
        "keys": a["peer_sub_keys"][0].reshape(SIDES, KEYS, P).transpose(2, 0, 1),
        "params": params, "consts": shape_constants(),
        "gain_ffn": a["norm_ffn"], "gain_final": a["norm_final"][None, :],
        "peer_down": a["peer_down"][0], "peer_up": a["peer_up"][0],
    }
    return {k: np.ascontiguousarray(v) for k, v in out.items()}


def program(nc, arrays):
    args = [nc.dram_tensor(n, arrays[n].shape, FP32, kind="ExternalInput").ap() for n in _INS]
    args += [nc.dram_tensor(n, shape, FP32, kind="ExternalOutput").ap() for n, shape in _OUTS]
    build(nc, *args)
    return nc


def kernel(**inputs):
    import concourse.bacc as bacc
    from concourse.bass_utils import run_bass_kernel_spmd
    arrays = lay_out(inputs)
    nc = program(bacc.Bacc("TRN2", target_bir_lowering=False, num_devices=1), arrays)
    r = run_bass_kernel_spmd(nc, [arrays], core_ids=[0]).results[0]
    ret = [r[n].transpose(1, 0, 2)[None, None] for n in ("ret_prompt", "ret_sample")]
    conv = [r[n].transpose(2, 1, 0).reshape(1, 1, PAD, CW) for n in ("conv_prompt", "conv_sample")]
    return (r["y_prompt"][None], r["y_sample"][None], ret[0], ret[1], conv[0], conv[1])
```

```python
import math
from contextlib import ExitStack

import numpy as np
import concourse.bass as bass
from concourse import mybir

FP32 = mybir.dt.float32
U32 = mybir.dt.uint32
ALU = mybir.AluOpType
ACT = mybir.ActivationFunctionType
AX = mybir.AxisListType

P = 128
D = 1024
KD = D // P
SEQ, DEC = 512, 32
T = SEQ + DEC
TILES = SEQ // P + 1
ROWS = [P] * (SEQ // P) + [DEC]
SAMPLE = TILES - 1
PAST = 256
HEADS, HD = 4, 128
RW = HEADS * HD
CW = D - RW
CT = CW // P
TAPS = 31
PAD = TAPS - 1
SEC = 512
SECTIONS = (4 * RW + 2 * CW + D + 2048) // SEC
S_Q, S_K, S_V, S_G, S_A, S_B, S_OUT, S_QUERY = 0, 1, 2, 3, 4, 5, 6, 8
WEIGHT_ORDER = [S_A, S_B, S_Q, S_K, S_G, S_V, S_OUT, S_OUT + 1] + [S_QUERY + i for i in range(4)]
WSLOTS = 3
PH, KEYS, TOPK = 8, 128, 16
EXPERTS = KEYS * KEYS
SIDES = 2 * PH
FOLDED = P // DEC
VT = (TILES - 1) * PH + PH // FOLDED
EPS = 1e-6
LOWEST = -3.0e38
SLOTS = 12
GROUP = 4
GROUPS = TOPK // GROUP
DIAGS = 8


def shape_constants():
    f = np.float32
    half = HD // 2
    inv = (f(10000.0) ** (-np.arange(half, dtype=f) / f(half))).astype(f)
    pos = np.concatenate([np.arange(SEQ, dtype=f), f(PAST) + np.arange(DEC, dtype=f)])
    ang = (pos[:, None] * inv[None, :]).astype(f).astype(np.float64)
    trig = np.zeros((P, TILES, 2, half), f)
    for t in range(TILES):
        r = ROWS[t]
        trig[:r, t, 0] = np.cos(ang[t * P:t * P + r])
        trig[:r, t, 1] = np.sin(ang[t * P:t * P + r])
    log_gamma = np.log1p(-np.exp2(-5.0 - np.arange(HEADS)))
    i = np.arange(P)
    diff = i[None, :] - i[:, None]
    scale = HD ** -0.5
    decay = np.zeros((P, HEADS, P), f)
    cross = np.zeros((P, HEADS, P), f)
    key_decay = np.zeros((P, 2, HEADS), f)
    for h in range(HEADS):
        decay[:, h] = np.where(diff >= 0, np.exp(log_gamma[h] * np.maximum(diff, 0)), 0.0) * scale
        cross[:, h] = np.exp(log_gamma[h] * (i + 1.0))[None, :]
        key_decay[:, 0, h] = np.exp(log_gamma[h] * (P - 1.0 - i)) * scale
        key_decay[:DEC, 1, h] = np.exp(log_gamma[h] * (DEC - 1.0 - i[:DEC])) * scale
    ident = np.eye(P, dtype=f)
    fold = (np.arange(P)[:, None] % DEC == np.arange(P)[None, :]).astype(f)
    iota = np.broadcast_to(np.arange(TOPK, dtype=f), (P, TOPK))
    parts = [trig.reshape(P, -1), decay.reshape(P, -1), cross.reshape(P, -1), key_decay.reshape(P, -1),
             ident, fold, iota]
    return np.concatenate(parts, axis=1).astype(f)


C_TRIG = 0
C_DECAY = C_TRIG + TILES * HD
C_CROSS = C_DECAY + HEADS * P
C_KDEC = C_CROSS + HEADS * P
C_IDENT = C_KDEC + 2 * HEADS
C_FOLD = C_IDENT + P
C_IOTA = C_FOLD + P
C_WIDTH = C_IOTA + TOPK
G_MIX = 0
G_RET = G_MIX + KD
G_BIAS = G_RET + HEADS
G_LNG = G_BIAS + CT
G_LNB = G_LNG + CT
G_TAPS = G_LNB + CT
G_WIDTH = G_TAPS + CT * TAPS


def gammas(length):
    return [float(np.exp(np.log1p(-np.exp2(-5.0 - h)) * length)) for h in range(HEADS)]


def retention_schedule():
    def head(t):
        return [("ret_qT", t), ("ret_kT", t)] if t < TILES else []

    def out(t):
        return [("ret_out", t), ("ret_state", t)] if 0 <= t else []

    def scores(t):
        return [("ret_scores", t)] if t < TILES else []

    def back(t):
        return [("ret_yT", t)] if 0 <= t else []
    v = [[("qkvg", S_V, t)] for t in range(TILES)]
    order = v[0] + [("ln_mean", 0), ("ln_mean", 1)] + head(0) + v[1] + [("ln_var", 0), ("ln_var", 1)] + scores(0) + v[2]
    for t in range(1, TILES + 1):
        order += head(t) + out(t - 1) + scores(t) + back(t - 1)
        if t + 2 < TILES:
            order += v[t + 2]
    return order


def psum_jobs():
    jobs = [(("norm_t", t, i), "dve") for t in range(TILES) for i in range(2)]
    for s in (S_A, S_B):
        jobs += [(("glu", s, c), "act") for c in range(CT + 1)]
    for s in (S_Q, S_K, S_G):
        jobs += [(("qkvg", s, t), "act") for t in range(TILES)]
    jobs += [(name, "act" if name[0] == "qkvg" else "dve") for name in retention_schedule()]
    for t in range(TILES):
        jobs += [(("mix_out", t, i), "dve") for i in range(2)]
    jobs += [(("ffn_t", t, i), "act") for t in range(TILES) for i in range(2)]
    for hs in range(SIDES + 1):
        if hs < SIDES:
            jobs += [(("query", hs, 0), "act"), (("query", hs, 1), "act")]
        if hs:
            jobs += [(("scores", hs - 1), "dve")]
    return jobs


JOBS = psum_jobs()
JOB = {name: n for n, (name, _) in enumerate(JOBS)}
EMPTIED = {}
_seen = {"dve": 0, "act": 0}
for _name, _by in JOBS:
    _seen[_by] += 1
    EMPTIED[_name] = _seen[_by]
BANKS = 7


def build(nc, x_prompt, x_sample, state_ret, conv_state, weights, keys, params, consts, gain_ffn, gain_final,
          experts, y_prompt, y_sample, ret_prompt, ret_sample, conv_prompt, conv_sample):
    ctx = ExitStack()
    with ctx:
        def sb(name, shape, dt=FP32):
            return ctx.enter_context(nc.sbuf_tensor(name, shape, dt))

        def sem(name):
            return ctx.enter_context(nc.semaphore(name))

        arena = sb("arena", [P, SLOTS * 2 * D])
        w_ring = arena[:, 0:WSLOTS * KD * SEC].rearrange("p (s k n) -> p s k n", s=WSLOTS, k=KD)
        z_at = WSLOTS * KD * SEC
        z = arena[:, z_at:z_at + TILES * 4 * SEC].rearrange("p (t s n) -> p t s n", t=TILES, s=4)
        key_at = z_at + TILES * 4 * SEC
        keysT = arena[:, key_at:key_at + SIDES * KEYS].rearrange("p (s n) -> p s n", s=SIDES)
        queryT = arena[:, z_at:z_at + 4 * T].rearrange("p (b t) -> p b t", b=4)
        ring = arena[:, :].rearrange("p (s d) -> p s d", s=SLOTS)

        xs = sb("xs", [P, TILES, D])
        hn = sb("hn", [P, TILES, D])
        scratch = hn[:, :, :].rearrange("p t d -> p (t d)")

        def scratch4(n):
            return scratch[:, n * RW:(n + 1) * RW].rearrange("p (h d) -> p h d", h=HEADS)
        q_rot, k_rot, k_dec, qT, kT, sc_dec, o_norm = (scratch4(n) for n in range(7))
        qT_cross = [scratch4(7), scratch4(8)]
        hT = sb("hT", [P, KD, T])
        loop_mem = hT[:, :, :].rearrange("p k t -> p (k t)")
        diag = loop_mem[:, 0:DIAGS * P].rearrange("p (k n) -> p k n", k=DIAGS)
        row_now = loop_mem[:, DIAGS * P:DIAGS * P + D]
        product = loop_mem[:, DIAGS * P + D:DIAGS * P + 2 * D]
        region_b = sb("region_b", [P, KD * T + CT * (SEQ + PAD + DEC + PAD) + CT * T])
        yT = region_b[:, 0:KD * T].rearrange("p (k t) -> p k t", k=KD)
        at = KD * T
        u_p = region_b[:, at:at + CT * (SEQ + PAD)].rearrange("p (c t) -> p c t", c=CT)
        conv_part = region_b[:, HEADS * T:KD * T]
        gate_tanh = conv_part[:, 0:2 * RW].rearrange("p (b n) -> p b n", b=2)
        deviation, newton = conv_part[:, 0:T], conv_part[:, T:2 * T]
        row_gain = region_b[:, at:at + D]
        at += CT * (SEQ + PAD)
        u_s = region_b[:, at:at + CT * (DEC + PAD)].rearrange("p (c t) -> p c t", c=CT)
        at += CT * (DEC + PAD)
        conv = region_b[:, at:at + CT * T].rearrange("p (c t) -> p c t", c=CT)
        scores = region_b[:, 0:VT * 2 * KEYS].rearrange("p (v s n) -> p v s n", v=VT, s=2)

        cst = sb("cst", [P, C_WIDTH])
        par = sb("par", [P, G_WIDTH])
        half_ln = sb("half_ln", [P, 2 * CT])
        state = sb("state", [P, 2, HEADS, HD])
        ones_cw = sb("ones_cw", [P, P])
        neg_half = sb("neg_half", [P, 1])
        sq_sum = sb("sq_sum", [P, 3 * TILES])
        rstd = sb("rstd", [P, 3 * TILES])
        bn = sb("bn", [P, HEADS, 6])
        mv = sb("mv", [P, HEADS, 2])
        ret_rstd = sb("ret_rstd", [P, HEADS])
        var = sb("var", [P, T])
        rot_tmp = sb("rot_tmp", [P, HEADS, HD // 2])

        flat_state = state[:, :, :, :].rearrange("p w h d -> p (w h d)")
        sc_now = flat_state[:, 0:2 * KEYS].rearrange("p (s n) -> p s n", s=2)
        cand = flat_state[:, 2 * KEYS:2 * KEYS + TOPK * TOPK]
        cand_cut = flat_state[:, 2 * KEYS + TOPK * TOPK:2 * KEYS + 2 * TOPK * TOPK]
        picks = cst[:, C_TRIG:C_TRIG + 2 * TOPK * TOPK].rearrange("p (s a b) -> p s a b", s=2, a=TOPK)

        trig = cst[:, C_TRIG:C_DECAY].rearrange("p (t c n) -> p t c n", t=TILES, c=2)
        decay = cst[:, C_DECAY:C_CROSS].rearrange("p (h n) -> p h n", h=HEADS)
        cross = cst[:, C_CROSS:C_KDEC].rearrange("p (h n) -> p h n", h=HEADS)
        key_decay = cst[:, C_KDEC:C_IDENT].rearrange("p (c h) -> p c h", c=2)
        ident = cst[:, C_IDENT:C_FOLD]
        fold = cst[:, C_FOLD:C_IOTA]
        iota = cst[:, C_IOTA:C_WIDTH]

        sc_cut = var[:, 0:2 * KEYS].rearrange("p (s n) -> p s n", s=2)
        top_s = sb("top_s", [P, 2, TOPK])
        top_i = sb("top_i", [P, 2, TOPK], U32)
        top_f = sb("top_f", [P, 2, TOPK])
        best_s = sb("best_s", [P, TOPK])
        best_i = sb("best_i", [P, TOPK], U32)
        pair_i = sb("pair_i", [P, 2, TOPK], U32)
        pair_f = sb("pair_f", [P, 2, TOPK])
        picked = sb("picked", [P, 2, TOPK])
        expert_f = sb("expert_f", [P, TOPK])
        expert = sb("expert", [P, 3, TOPK], U32)
        neg_max = sb("neg_max", [P, 3])
        best_kept = sb("best_kept", [P, 3, TOPK])
        gate = sb("gate", [P, 3, TOPK])
        gate_sum = sb("gate_sum", [P, 3])
        dots = sb("dots", [P, TOPK])
        gl = sb("gl", [P, 3, GROUP])
        gl_tanh = sb("gl_tanh", [P, GROUP])
        weight = sb("weight", [P, 2, GROUP])

        ps = ctx.enter_context(nc.psum_tensor("ps", [P, 8, SEC], FP32))
        product_ps = ps[:, 6:8, :].rearrange("p b n -> p (b n)")
        sample_scores = ps[:, 7, :].rearrange("p (v s n) -> p v s n", v=2, s=2)

        def bank(name):
            return ps[:, JOB[name] % BANKS, :]

        s_x = sem("s_x")
        s_cst = sem("s_cst")
        s_par = sem("s_par")
        s_w = [sem(f"s_w{i}") for i in range(WSLOTS)]
        s_keys = sem("s_keys")
        s_gain = sem("s_gain")
        s_gain2 = sem("s_gain2")
        s_st = sem("s_st")
        s_pe = sem("s_pe")
        s_by = {"dve": sem("s_by_dve"), "act": sem("s_by_act")}
        s_setup = sem("s_setup")
        s_sq = sem("s_sq")
        s_rstd = sem("s_rstd")
        s_hn = sem("s_hn")
        s_wsec = sem("s_wsec")
        s_u = sem("s_u")
        s_conv = sem("s_conv")
        s_convout = sem("s_convout")
        s_gt = sem("s_gt")
        s_gate = sem("s_gate")
        s_csq = sem("s_csq")
        s_dev = sem("s_dev")
        s_yh = sem("s_yh")
        s_yt = sem("s_yt")
        s_yconv = sem("s_yconv")
        s_rot = sem("s_rot")
        s_kdec = sem("s_kdec")
        s_retout = sem("s_retout")
        s_ostat = sem("s_ostat")
        s_orstd = sem("s_orstd")
        s_on = sem("s_on")
        s_rep = sem("s_rep")
        s_ss = sem("s_ss")
        s_scores = sem("s_scores")
        s_out = sem("s_out")
        s_idx = sem("s_idx")
        s_exp = sem("s_exp")
        s_slot = [sem(f"s_slot{i}") for i in range(SLOTS)]
        s_used = sem("s_used")
        s_poly = sem("s_poly")
        s_tanh = sem("s_tanh")
        s_wt = sem("s_wt")
        s_diag = sem("s_diag")
        s_acc = sem("s_acc")
        s_yout = sem("s_yout")

        def sections_used(s):
            return WEIGHT_ORDER.index(s) + 1

        block = ctx.enter_context(nc.Block())

        @block.sync
        def _(sp):
            sp.dma_start(xs[:, 0:SAMPLE, :], x_prompt.rearrange("(t p) d -> p t d", p=P)).then_inc(s_x, 16)
            sp.dma_start(xs[0:DEC, SAMPLE, :], x_sample).then_inc(s_x, 16)
            sp.dma_start(par[:, :], params).then_inc(s_par, 16)
            sp.dma_start(cst[:, :], consts).then_inc(s_cst, 16)
            for n, s in enumerate(WEIGHT_ORDER):
                if n >= WSLOTS:
                    sp.wait_ge(s_wsec, n - WSLOTS + 1)
                sp.dma_start(w_ring[:, n % WSLOTS], weights[s]).then_inc(s_w[n % WSLOTS], 16)
                if n == 0:
                    sp.dma_start(u_s[:, :, 0:PAD], conv_state).then_inc(s_st, 16)
                    sp.dma_start(state[:, 1], state_ret).then_inc(s_st, 16)
                    sp.dma_start(keysT, keys).then_inc(s_keys, 16)
                if WEIGHT_ORDER[n] == S_OUT + 1:
                    sp.wait_ge(s_u, 1)
                    sp.dma_start(conv_prompt, u_p[:, :, SEQ:SEQ + PAD]).then_inc(s_convout, 16)
                    sp.dma_start(conv_sample, u_s[:, :, DEC:DEC + PAD]).then_inc(s_convout, 16)
                    sp.wait_ge(s_convout, 32)
                    sp.wait_ge(s_conv, 1)
                    sp.dma_start(row_gain, gain_ffn.to_broadcast([P, D])).then_inc(s_gain, 16)
                if WEIGHT_ORDER[n] == S_QUERY:
                    sp.wait_ge(s_by["dve"], EMPTIED[("ret_state", SAMPLE)])
                    sp.dma_start(ret_prompt, state[:, 0]).then_inc(s_retout, 16)
                    sp.dma_start(ret_sample, state[:, 1]).then_inc(s_retout, 16)
            sp.wait_ge(s_hn, 2 * TILES)
            for j in range(1, FOLDED):
                sp.dma_start(hn[j * DEC:(j + 1) * DEC, SAMPLE, :], hn[0:DEC, SAMPLE, :]).then_inc(s_rep, 16)
            sp.wait_ge(s_idx, VT)
            sp.dma_start(row_gain, gain_final.to_broadcast([P, D])).then_inc(s_gain2, 16)
            for t in range(TILES):
                sp.wait_ge(s_yout, t + 1)
                out = y_prompt[t * P:(t + 1) * P, :] if t < SAMPLE else y_sample
                sp.dma_start(out, xs[0:ROWS[t], t, :]).then_inc(s_out, 16)
            sp.wait_ge(s_out, 16 * TILES)
            sp.wait_ge(s_convout, 32)
            sp.wait_ge(s_retout, 32)

        @block.gpsimd
        def _(pool):
            nc.gpsimd.memset(neg_half[:, :], -0.5)
            pool.drain()

            def inverse_root(out, in_, rows, n, ready):
                nc.gpsimd.tensor_scalar(out=out, in0=in_, scalar1=1.0 / n, scalar2=EPS, op0=ALU.mult, op1=ALU.add)
                pool.drain()
                width = out.shape[-1]
                power = neg_half[0:rows, 0:1]
                nc.gpsimd.tensor_tensor(out=out, in0=out, in1=power if width == 1 else power.to_broadcast([rows, width]),
                                        op=ALU.pow).then_inc(ready, 1)

            for t in range(TILES):
                pool.wait_ge(s_sq, t + 1)
                inverse_root(rstd[0:ROWS[t], t:t + 1], sq_sum[0:ROWS[t], t:t + 1], ROWS[t], D, s_rstd)

            half = HD // 2
            pool.wait_ge(s_cst, 16)

            def retention_root(t):
                pool.wait_ge(s_ostat, t + 1)
                inverse_root(ret_rstd[0:ROWS[t], :], mv[0:ROWS[t], :, 1], ROWS[t], 1, s_orstd)

            for t in range(TILES):
                r = ROWS[t]
                pool.wait_ge(s_by["act"], EMPTIED[("qkvg", S_K, t)])
                if t:
                    pool.wait_ge(s_pe, JOB[("ret_kT", t - 1)] + 1)
                cos = trig[0:r, t, 0].unsqueeze(1).to_broadcast([r, HEADS, half])
                sin = trig[0:r, t, 1].unsqueeze(1).to_broadcast([r, HEADS, half])
                tmp = rot_tmp[0:r]
                for col, dst in ((0, q_rot), (1, k_rot)):
                    src = z[0:r, t, col].rearrange("p (h d) -> p h d", h=HEADS)
                    x1, x2 = src[:, :, 0:half], src[:, :, half:HD]
                    for a, b, o, op in ((x1, x2, dst[0:r, :, 0:half], ALU.subtract),
                                        (x2, x1, dst[0:r, :, half:HD], ALU.add)):
                        nc.gpsimd.tensor_tensor(out=o, in0=a, in1=cos, op=ALU.mult)
                        nc.gpsimd.tensor_tensor(out=tmp, in0=b, in1=sin, op=ALU.mult)
                        pool.drain()
                        nc.gpsimd.tensor_tensor(out=o, in0=o, in1=tmp, op=op)
                        pool.drain()
                pool.drain().then_inc(s_rot, 1)
                if t:
                    retention_root(t - 1)
                    pool.wait_ge(s_pe, JOB[("ret_state", t - 1)] + 1)
                kd = key_decay[0:r, 1 if t == SAMPLE else 0].unsqueeze(2).to_broadcast([r, HEADS, HD])
                nc.gpsimd.tensor_tensor(out=k_dec[0:r], in0=k_rot[0:r], in1=kd, op=ALU.mult).then_inc(s_kdec, 1)
            retention_root(SAMPLE)
            for t in range(TILES):
                pool.wait_ge(s_sq, TILES + t + 1)
                c = TILES + t
                inverse_root(rstd[0:ROWS[t], c:c + 1], sq_sum[0:ROWS[t], c:c + 1], ROWS[t], D, s_rstd)

            def gathers(triple, m, first=False):
                vt = triple * 3 + m
                pool.wait_ge(s_idx, vt + 1)
                pool.nop(nofuse=True)
                for k in range(TOPK):
                    slot = (m * TOPK + k) % SLOTS
                    if not first or k >= SLOTS:
                        pool.wait_ge(s_used, vt * TOPK + (k - SLOTS + 1))
                        pool.nop(nofuse=True)
                    pool.indirect_dma_start(ring[:, slot, :], None, experts,
                                            bass.IndirectOffsetOnAxis(ap=expert[:, m, k:k + 1], axis=0))\
                        .then_inc(s_slot[slot], 16)

            def final_root(t):
                pool.wait_ge(s_sq, 2 * TILES + t + 1)
                c = 2 * TILES + t
                inverse_root(rstd[0:ROWS[t], c:c + 1], sq_sum[0:ROWS[t], c:c + 1], ROWS[t], D, s_rstd)

            pool.wait_ge(s_scores, 1)
            for m in range(3):
                gathers(0, m, first=m == 0)
            with pool.Fori(1, VT // 3 - 1) as triple:
                for m in range(3):
                    gathers(triple, m)
            for vt in range(VT - 4, VT):
                gathers(vt // 3, vt % 3)
            for t in range(TILES):
                final_root(t)

        @block.scalar
        def _(act):
            def square_sum(src, col, rows, junk):
                nc.scalar.activation(junk, src, ACT.Square, accum_out=sq_sum[0:rows, col:col + 1]).then_inc(s_sq, 1)

            def emptied(ins):
                ins.then_inc(s_by["act"], 1)

            def filled(name):
                act.wait_ge(s_pe, JOB[name] + 1)

            act.wait_ge(s_x, 32)
            for t in range(TILES):
                square_sum(xs[0:ROWS[t], t], t, ROWS[t], hn[0:ROWS[t], t])
            for s in (S_A, S_B):
                func, scale = (ACT.Copy, 0.5) if s == S_A else (ACT.Tanh, 0.5)
                for c in range(CT + 1):
                    filled(("glu", s, c))
                    src = bank(("glu", s, c))
                    if c < CT:
                        dst = u_p[:, c, PAD:PAD + SEQ] if s == S_A else conv[:, c, 0:SEQ]
                    else:
                        src = src[:, 0:CT * DEC].rearrange("p (c t) -> p c t", c=CT)
                        dst = u_s[:, :, PAD:PAD + DEC] if s == S_A else conv[:, :, SEQ:T]
                    emptied(nc.scalar.activation(dst, src, func, scale=scale))

            def rows_in(s, t):
                r = ROWS[t]
                filled(("qkvg", s, t))
                src = bank(("qkvg", s, t))[0:r]
                if s == S_G:
                    if t >= 2:
                        act.wait_ge(s_gate, t - 1)
                    nc.scalar.activation(gate_tanh[0:r, t % 2], src, ACT.Tanh, scale=0.5)
                    emptied(nc.scalar.activation(z[0:r, t, s], src, ACT.Copy, scale=0.5))
                else:
                    emptied(nc.scalar.activation(z[0:r, t, s], src, ACT.Copy))

            for s in (S_Q, S_K, S_G):
                for t in range(TILES):
                    rows_in(s, t)
            rows_in(S_V, 0)
            act.wait_ge(s_by["dve"], EMPTIED[("ln_mean", 1)])
            for c in range(CT):
                nc.scalar.activation(yT[:, HEADS + c, :], conv[:, c, :], ACT.Square).then_inc(s_csq, 1)
            rows_in(S_V, 1)
            act.wait_ge(s_by["dve"], EMPTIED[("ln_var", 1)])
            nc.scalar.activation(deviation, var[:, :], ACT.Sqrt).then_inc(s_dev, 1)
            rows_in(S_V, 2)
            act.wait_ge(s_yh, 1)
            for c in range(CT):
                nc.scalar.activation(yT[:, HEADS + c, :], conv[:, c, :], ACT.Tanh).then_inc(s_yt, 1)
            rows_in(S_V, 3)
            rows_in(S_V, 4)
            for t in range(TILES):
                act.wait_ge(s_by["dve"], EMPTIED[("mix_out", t, 1)])
                square_sum(xs[0:ROWS[t], t], TILES + t, ROWS[t], hn[0:ROWS[t], t])
            for t in range(TILES):
                for i in range(2):
                    name = ("ffn_t", t, i)
                    filled(name)
                    r = ROWS[t]
                    src = bank(name).rearrange("p (k t) -> p k t", k=4)[:, :, 0:r]
                    emptied(nc.scalar.activation(hT[:, 4 * i:4 * i + 4, t * P:t * P + r], src, ACT.Copy))
            for hs in range(SIDES):
                for i in range(2):
                    name = ("query", hs, i)
                    filled(name)
                    if i == 0 and hs >= 4:
                        act.wait_ge(s_pe, JOB[("scores", hs - 4)] + 1)
                    lo, hi = (0, SEQ) if i == 0 else (SEQ, T)
                    emptied(nc.scalar.activation(queryT[:, hs % 4, lo:hi], bank(name)[:, 0:hi - lo], ACT.Copy))

            def head_tile(triple, m, base):
                vt = triple * 3 + m
                act.wait_ge(s_idx, vt + 1)
                act.nop(nofuse=True)
                nc.scalar.activation(gate[:, m, :], best_kept[:, m, :], ACT.Exp, bias=neg_max[:, m:m + 1],
                                     accum_out=gate_sum[:, m:m + 1]).then_inc(s_exp, 1)
                for g in range(GROUPS):
                    group = vt * GROUPS + g
                    act.wait_ge(s_poly, group + 1)
                    nc.scalar.activation(gl_tanh[:, :], gl[:, 2, :], ACT.Tanh, scale=math.sqrt(2.0 / math.pi))\
                        .then_inc(s_tanh, 1)
                    act.wait_ge(s_wt, group + 1)
                    act.nop(nofuse=True)
                    for i in range(GROUP):
                        k = g * GROUP + i
                        if not (isinstance(vt, int) and vt == 0 and k < DIAGS):
                            act.wait_ge(s_used, vt * TOPK + (k - DIAGS + 1))
                        nc.scalar.activation(diag[:, k % DIAGS, :], base, ACT.Copy, scale=weight[:, g % 2, i:i + 1])\
                            .then_inc(s_diag, 1)

            for m in range(3):
                head_tile(0, m, ident)
            with act.Fori(1, VT // 3 - 1) as triple:
                for m in range(3):
                    head_tile(triple, m, ident)
            for vt in range(VT - 4, VT):
                head_tile(vt // 3, vt % 3, ident if vt < VT - 2 else fold)
                if vt == VT - 2:
                    act.wait_ge(s_acc, VT - 2)
                    for t in range(SAMPLE):
                        square_sum(xs[0:ROWS[t], t], 2 * TILES + t, ROWS[t], hn[0:ROWS[t], t])
            act.wait_ge(s_acc, VT)
            square_sum(xs[0:DEC, SAMPLE], 2 * TILES + SAMPLE, DEC, hn[0:DEC, SAMPLE])

        @block.vector
        def _(dve):
            v = nc.vector

            def emptied(ins):
                ins.then_inc(s_by["dve"], 1)

            def filled(name):
                dve.wait_ge(s_pe, JOB[name] + 1)

            v.memset(ones_cw[:, :], 1.0 / CW)
            v.memset(u_p[:, :, 0:PAD], 0.0).then_inc(s_setup, 1)
            dve.wait_ge(s_par, 16)
            v.tensor_scalar(out=half_ln[:, :], in0=par[:, G_LNG:G_TAPS], scalar1=0.5, scalar2=None, op0=ALU.mult)
            for t in range(TILES):
                r = ROWS[t]
                dve.wait_ge(s_rstd, t + 1)
                v.tensor_scalar(out=hn[0:r, t], in0=xs[0:r, t], scalar1=rstd[0:r, t:t + 1], scalar2=None,
                                op0=ALU.mult).then_inc(s_hn, 1)
            for t in range(TILES):
                r = ROWS[t]
                for i in range(2):
                    name = ("norm_t", t, i)
                    filled(name)
                    src = bank(name).rearrange("p (k t) -> p k t", k=4)[:, :, 0:r]
                    gain = par[:, G_MIX + 4 * i:G_MIX + 4 * i + 4].unsqueeze(2).to_broadcast([P, 4, r])
                    emptied(v.tensor_tensor(out=hT[:, 4 * i:4 * i + 4, t * P:t * P + r], in0=src, in1=gain,
                                            op=ALU.mult))
            dve.wait_ge(s_by["act"], EMPTIED[("glu", S_B, CT)])
            dve.wait_ge(s_st, 32)
            for c in range(CT):
                v.scalar_tensor_tensor(out=u_p[:, c, PAD:PAD + SEQ], in0=conv[:, c, 0:SEQ], scalar=1.0,
                                       in1=u_p[:, c, PAD:PAD + SEQ], op0=ALU.add, op1=ALU.mult)
            v.scalar_tensor_tensor(out=u_s[:, :, PAD:PAD + DEC], in0=conv[:, :, SEQ:T], scalar=1.0,
                                   in1=u_s[:, :, PAD:PAD + DEC], op0=ALU.add, op1=ALU.mult).then_inc(s_u, 1)
            dve.drain()
            for j in range(TAPS):
                for c in range(CT):
                    tap = par[:, G_TAPS + c * TAPS + j:G_TAPS + c * TAPS + j + 1]
                    for src, lo, n in ((u_p, 0, SEQ), (u_s, SEQ, DEC)):
                        out = conv[:, c, lo:lo + n]
                        if j == 0:
                            v.tensor_scalar(out=out, in0=src[:, c, 0:n], scalar1=tap,
                                            scalar2=par[:, G_BIAS + c:G_BIAS + c + 1], op0=ALU.mult, op1=ALU.add)
                        else:
                            last = v.scalar_tensor_tensor(out=out, in0=src[:, c, j:j + n], scalar=tap, in1=out,
                                                          op0=ALU.mult, op1=ALU.add)
                if j < TAPS - 1:
                    dve.drain()
            last.then_inc(s_conv, 1)
            for t in range(TILES):
                r = ROWS[t]
                dve.wait_ge(s_by["act"], EMPTIED[("qkvg", S_G, t)])
                v.scalar_tensor_tensor(out=z[0:r, t, S_G], in0=gate_tanh[0:r, t % 2], scalar=1.0, in1=z[0:r, t, S_G],
                                       op0=ALU.add, op1=ALU.mult).then_inc(s_gate, 1)
            def mean_off():
                for i, (lo, hi) in enumerate(((0, SEQ), (SEQ, T))):
                    filled(("ln_mean", i))
                    mean = bank(("ln_mean", i))[:, 0:hi - lo].unsqueeze(1).to_broadcast([P, CT, hi - lo])
                    emptied(v.tensor_tensor(out=conv[:, :, lo:hi], in0=conv[:, :, lo:hi], in1=mean, op=ALU.subtract))

            def variance():
                for i, (lo, hi) in enumerate(((0, SEQ), (SEQ, T))):
                    filled(("ln_var", i))
                    emptied(v.tensor_scalar(out=var[:, lo:hi], in0=bank(("ln_var", i))[:, 0:hi - lo], scalar1=EPS,
                                            scalar2=None, op0=ALU.add))

            def conv_norm():
                dve.wait_ge(s_dev, 1)
                v.reciprocal(deviation, deviation)
                dve.drain()
                v.tensor_tensor(out=newton, in0=deviation, in1=deviation, op=ALU.mult)
                dve.drain()
                v.tensor_tensor(out=newton, in0=newton, in1=var[:, :], op=ALU.mult)
                dve.drain()
                v.tensor_scalar(out=newton, in0=newton, scalar1=-0.5, scalar2=1.5, op0=ALU.mult, op1=ALU.add)
                dve.drain()
                v.tensor_tensor(out=var[:, :], in0=newton, in1=deviation, op=ALU.mult)
                dve.drain()
                v.tensor_tensor(out=conv[:, :, :], in0=conv[:, :, :],
                                in1=var[:, :].unsqueeze(1).to_broadcast([P, CT, T]), op=ALU.mult)
                dve.drain()
                for c in range(CT):
                    last = v.tensor_scalar(out=conv[:, c, :], in0=conv[:, c, :], scalar1=half_ln[:, c:c + 1],
                                           scalar2=half_ln[:, CT + c:CT + c + 1], op0=ALU.mult, op1=ALU.add)
                last.then_inc(s_yh, 1)

            def conv_silu():
                dve.wait_ge(s_yt, CT)
                v.scalar_tensor_tensor(out=yT[:, HEADS:KD, :], in0=yT[:, HEADS:KD, :], scalar=1.0, in1=conv[:, :, :],
                                       op0=ALU.add, op1=ALU.mult).then_inc(s_yconv, 1)

            def four(name, n):
                return bank(name).rearrange("p (h n) -> p h n", h=HEADS)[:, :, 0:n]

            def ret_step(kind, t):
                name = (kind, t)
                r = ROWS[t]
                filled(name)
                if kind == "ret_qT":
                    v.tensor_copy(qT[:, :, 0:r], four(name, r))
                    emptied(v.tensor_tensor(out=qT_cross[t % 2][:, :, 0:r], in0=four(name, r), in1=cross[:, :, 0:r],
                                            op=ALU.mult))
                elif kind == "ret_kT":
                    emptied(v.tensor_copy(kT[:, :, 0:r], four(name, r)))
                elif kind == "ret_scores":
                    emptied(v.tensor_tensor(out=sc_dec[0:r, :, 0:r], in0=four(name, r)[0:r], in1=decay[0:r, :, 0:r],
                                            op=ALU.mult))
                elif kind == "ret_out":
                    o = four(name, HD)[0:r]
                    for h in range(HEADS):
                        v.bn_stats(bn[0:r, h, :], o[:, h, :])
                    dve.drain()
                    for h in range(HEADS):
                        last = v.bn_aggr(mv[0:r, h, :], bn[0:r, h, :])
                    last.then_inc(s_ostat, 1)
                    dve.wait_ge(s_orstd, t + 1)
                    for h in range(HEADS):
                        last = v.tensor_scalar(out=o_norm[0:r, h, :], in0=o[:, h, :], scalar1=mv[0:r, h, 0:1],
                                               scalar2=ret_rstd[0:r, h:h + 1], op0=ALU.subtract, op1=ALU.mult)
                    emptied(last)
                    dve.drain()
                    v.tensor_tensor(out=o_norm[0:r], in0=o_norm[0:r],
                                    in1=z[0:r, t, S_G].rearrange("p (h d) -> p h d", h=HEADS), op=ALU.mult)\
                        .then_inc(s_on, 1)
                elif kind == "ret_state":
                    add = four(name, HD)
                    which, length = (1, DEC) if t == SAMPLE else (0, P)
                    if t == 0:
                        last = v.tensor_copy(state[:, 0], add)
                    else:
                        for h, g in enumerate(gammas(length)):
                            last = v.scalar_tensor_tensor(out=state[:, which, h], in0=state[:, which, h], scalar=g,
                                                          in1=add[:, h], op0=ALU.mult, op1=ALU.add)
                    emptied(last)
                else:
                    gain = par[:, G_RET:G_RET + HEADS].unsqueeze(2).to_broadcast([P, HEADS, r])
                    emptied(v.tensor_tensor(out=yT[:, 0:HEADS, t * P:t * P + r], in0=four(name, r), in1=gain,
                                            op=ALU.mult))

            for name in retention_schedule():
                if name == ("ln_mean", 0):
                    mean_off()
                elif name == ("ln_var", 0):
                    variance()
                elif name[0].startswith("ret_"):
                    ret_step(*name)
                    if name == ("ret_scores", 0):
                        conv_norm()
                    elif name == ("ret_yT", 0):
                        conv_silu()
            for t in range(TILES):
                for i in range(2):
                    name = ("mix_out", t, i)
                    filled(name)
                    part = xs[0:ROWS[t], t, i * SEC:(i + 1) * SEC]
                    emptied(v.tensor_tensor(out=part, in0=bank(name)[0:ROWS[t]], in1=part, op=ALU.add))
            dve.wait_ge(s_gain, 16)
            for t in range(TILES):
                r = ROWS[t]
                dve.wait_ge(s_rstd, TILES + t + 1)
                v.scalar_tensor_tensor(out=hn[0:r, t], in0=xs[0:r, t], scalar=rstd[0:r, TILES + t:TILES + t + 1],
                                       in1=row_gain[0:r, :], op0=ALU.mult, op1=ALU.mult).then_inc(s_hn, 1)
            def top16(values, cut, best, index):
                v.max(best[:, 0:8], values)
                dve.drain()
                v.max_index(index[:, 0:8], best[:, 0:8], values)
                v.match_replace(cut, best[:, 0:8], values, LOWEST)
                dve.drain()
                v.max(best[:, 8:16], cut)
                dve.drain()
                v.max_index(index[:, 8:16], best[:, 8:16], cut)

            def choose(vt, u, between):
                between = list(between)

                def pause():
                    if between:
                        between.pop(0)()
                at = bass.ds(vt * 2 * KEYS, 2 * KEYS)
                v.tensor_copy(sc_now.rearrange("p s n -> p (s n)"), region_b[:, at])
                dve.drain()
                top16(sc_now[:, 0, :], sc_cut[:, 0, :], top_s[:, 0, :], top_i[:, 0, :])
                pause()
                top16(sc_now[:, 1, :], sc_cut[:, 1, :], top_s[:, 1, :], top_i[:, 1, :])
                dve.drain()
                v.tensor_copy(top_f[:, :, :], top_i[:, :, :])
                v.tensor_tensor(out=cand[:, :].rearrange("p (a b) -> p a b", a=TOPK),
                                in0=top_s[:, 0, :].unsqueeze(2).to_broadcast([P, TOPK, TOPK]),
                                in1=top_s[:, 1, :].unsqueeze(1).to_broadcast([P, TOPK, TOPK]), op=ALU.add)
                dve.drain()
                pause()
                top16(cand[:, :], cand_cut[:, :], best_s[:, :], best_i[:, :])
                dve.drain()
                pause()
                v.tensor_copy(best_kept[:, u, :], best_s[:, :])
                v.tensor_scalar(out=neg_max[:, u:u + 1], in0=best_s[:, 0:1], scalar1=-1.0, scalar2=None, op0=ALU.mult)
                v.tensor_scalar(out=pair_i[:, 0, :], in0=best_i[:, :], scalar1=4, scalar2=None,
                                op0=ALU.logical_shift_right)
                v.tensor_scalar(out=pair_i[:, 1, :], in0=best_i[:, :], scalar1=TOPK - 1, scalar2=None,
                                op0=ALU.bitwise_and)
                dve.drain()
                v.tensor_copy(pair_f[:, :, :], pair_i[:, :, :])
                dve.drain()
                for s in range(2):
                    v.tensor_tensor(out=picks[:, s], in0=pair_f[:, s, :].unsqueeze(2).to_broadcast([P, TOPK, TOPK]),
                                    in1=iota.unsqueeze(1).to_broadcast([P, TOPK, TOPK]), op=ALU.is_equal)
                dve.drain()
                for s in range(2):
                    v.tensor_tensor(out=picks[:, s], in0=picks[:, s],
                                    in1=top_f[:, s, :].unsqueeze(1).to_broadcast([P, TOPK, TOPK]), op=ALU.mult)
                dve.drain()
                v.tensor_reduce(out=picked[:, :, :], in_=picks[:, :, :, :], axis=AX.X, op=ALU.add)
                dve.drain()
                v.scalar_tensor_tensor(out=expert_f[:, :], in0=picked[:, 0, :], scalar=float(KEYS), in1=picked[:, 1, :],
                                       op0=ALU.mult, op1=ALU.add)
                dve.drain()
                v.tensor_copy(expert[:, u, :], expert_f[:, :]).then_inc(s_idx, 1)
                for rest in between:
                    rest()

            dve.wait_ge(s_retout, 32)
            by_head = scores[:, 0:SAMPLE * PH].rearrange("p (t h) s n -> p t h s n", t=SAMPLE)
            for hs in range(SIDES):
                name = ("scores", hs)
                filled(name)
                src = bank(name).rearrange("p (t n) -> p t n", t=SAMPLE)
                emptied(v.tensor_copy(by_head[:, :, hs // 2, hs % 2, :], src))
                if hs in (1, 3):
                    dve.drain()
                    choose(hs // 2, hs // 2, ())
            v.tensor_copy(scores[:, SAMPLE * PH:VT], sample_scores).then_inc(s_scores, 1)


            def soft(vt, m):
                dve.wait_ge(s_exp, vt + 1)
                dve.nop(nofuse=True)
                v.reciprocal(gate_sum[:, m:m + 1], gate_sum[:, m:m + 1])
                dve.drain()
                v.tensor_scalar(out=gate[:, m, :], in0=gate[:, m, :], scalar1=gate_sum[:, m:m + 1], scalar2=0.5,
                                op0=ALU.mult, op1=ALU.mult)

            def weigh(triple, m, g):
                group = triple * (3 * GROUPS) + (m * GROUPS + g)
                for i in range(GROUP):
                    place = (m * GROUPS + g) * GROUP + i
                    slot = place % SLOTS
                    dve.wait_ge(s_slot[slot], triple * 64 + 16 * (place // SLOTS + 1))
                    out = product if i % 2 else product_ps
                    v.tensor_tensor_reduce(out=out, in0=ring[:, slot, 0:D], in1=row_now, scale=1.0, scalar=0.0,
                                           op0=ALU.mult, op1=ALU.add, accum_out=dots[:, i:i + 1])
                    if i % 2:
                        dve.drain()
                x = dots[:, 0:GROUP]
                v.tensor_tensor(out=gl[:, 0, :], in0=x, in1=x, op=ALU.mult)
                v.tensor_tensor(out=gl[:, 1, :], in0=gate[:, m, g * GROUP:(g + 1) * GROUP], in1=x, op=ALU.mult)
                dve.drain()
                v.tensor_scalar(out=gl[:, 0, :], in0=gl[:, 0, :], scalar1=0.044715, scalar2=1.0, op0=ALU.mult,
                                op1=ALU.add)
                dve.drain()
                v.tensor_tensor(out=gl[:, 2, :], in0=gl[:, 0, :], in1=x, op=ALU.mult).then_inc(s_poly, 1)
                dve.wait_ge(s_tanh, group + 1)
                dve.nop(nofuse=True)
                v.scalar_tensor_tensor(out=weight[:, g % 2, :], in0=gl_tanh[:, :], scalar=1.0, in1=gl[:, 1, :],
                                       op0=ALU.add, op1=ALU.mult).then_inc(s_wt, 1)
                dve.drain()

            def add(vt, bank_pair, tile, rows):
                dve.wait_ge(s_used, (vt + 1) * TOPK)
                dve.nop(nofuse=True)
                part = xs[:, :, :].rearrange("p t d -> p (t d)")[0:rows, bass.ds(tile * D, D)]
                total = ps[0:rows, 2 * bank_pair:2 * bank_pair + 2, :].rearrange("p b n -> p (b n)")
                v.tensor_tensor(out=part, in0=total, in1=part, op=ALU.add).then_inc(s_acc, 1)
                dve.drain()

            def head_tile(triple, m, tile, before):
                vt = triple * 3 + m
                v.tensor_copy(row_now, hn[:, :, :].rearrange("p t d -> p (t d)")[:, bass.ds(tile * D, D)])
                soft(vt, m)
                dve.drain()

                def group(g):
                    return lambda: weigh(triple, m, g)
                group(0)()
                if before is not None:
                    add(vt - 1, (m + 2) % 3, *before)
                if isinstance(vt, int) and vt + 2 >= VT:
                    for g in range(1, GROUPS):
                        group(g)()
                else:
                    choose(vt + 2, (m + 2) % 3, [group(g) for g in range(1, GROUPS)])

            for m in range(3):
                head_tile(0, m, 0, (0, P) if m else None)
            with dve.Fori(1, VT // 3 - 1) as triple:
                for m in range(3):
                    vt = triple * 3 + m
                    head_tile(triple, m, vt >> 3, ((vt - 1) >> 3, P))
            head_tile(VT // 3 - 1, 0, SAMPLE - 1, (SAMPLE - 1, P))
            head_tile(VT // 3 - 1, 1, SAMPLE - 1, (SAMPLE - 1, P))
            dve.wait_ge(s_rep, 16 * (FOLDED - 1))
            head_tile(VT // 3 - 1, 2, SAMPLE, (SAMPLE - 1, P))
            head_tile(VT // 3, 0, SAMPLE, (SAMPLE, DEC))

            def final_norm(t):
                r = ROWS[t]
                dve.wait_ge(s_rstd, 2 * TILES + t + 1)
                v.scalar_tensor_tensor(out=xs[0:r, t], in0=xs[0:r, t], scalar=rstd[0:r, 2 * TILES + t:2 * TILES + t + 1],
                                       in1=row_gain[0:r, :], op0=ALU.mult, op1=ALU.mult).then_inc(s_yout, 1)

            dve.wait_ge(s_gain2, 16)
            for t in range(SAMPLE):
                final_norm(t)
            add(VT - 1, 0, SAMPLE, DEC)
            final_norm(SAMPLE)

        @block.tensor
        def _(pe):
            mm = nc.tensor.matmul

            def open_bank(name):
                n = JOB[name]
                if n >= BANKS:
                    before, by = JOBS[n - BANKS]
                    pe.wait_ge(s_by[by], EMPTIED[before])
                return bank(name)

            def done(ins):
                ins.then_inc(s_pe, 1)

            def section(s):
                n = WEIGHT_ORDER.index(s)
                pe.wait_ge(s_w[n % WSLOTS], 16 * (n // WSLOTS + 1))
                return w_ring[:, n % WSLOTS]

            pe.wait_ge(s_cst, 16)

            def transposes(name, sources, r):
                out = open_bank(name)
                for j, src in enumerate(sources):
                    last = nc.tensor.transpose(out[:, j * P:j * P + r], src, ident[0:r, 0:r])
                done(last)

            def row_transposes(kind, first):
                for t in range(TILES):
                    pe.wait_ge(s_hn, first + t + 1)
                    for i in range(2):
                        transposes((kind, t, i), [hn[0:ROWS[t], t, k * P:(k + 1) * P] for k in range(4 * i, 4 * i + 4)],
                                   ROWS[t])

            row_transposes("norm_t", 0)
            pe.wait_ge(s_by["dve"], EMPTIED[("norm_t", SAMPLE, 1)])
            for s in (S_A, S_B):
                w = section(s)
                for c in range(CT):
                    out = open_bank(("glu", s, c))
                    for k in range(KD):
                        last = mm(out, w[:, k, c * P:(c + 1) * P], hT[:, k, 0:SEQ], start=k == 0, stop=k == KD - 1)
                    done(last)
                out = open_bank(("glu", s, CT))
                for c in range(CT):
                    for k in range(KD):
                        last = mm(out[:, c * DEC:(c + 1) * DEC], w[:, k, c * P:(c + 1) * P], hT[:, k, SEQ:T],
                                  start=k == 0, stop=k == KD - 1)
                last.then_inc(s_pe, 1)
                pe.drain().then_inc(s_wsec, 1)

            def rows_times(name, lhs, w, r, lo):
                out = open_bank(name)
                for k in range(KD):
                    last = mm(out[0:r, :], lhs[:, k, lo:lo + r], w[:, k, :], start=k == 0, stop=k == KD - 1)
                done(last)

            for s in (S_Q, S_K, S_G):
                w = section(s)
                for t in range(TILES):
                    rows_times(("qkvg", s, t), hT, w, ROWS[t], t * P)
                pe.drain().then_inc(s_wsec, 1)

            def channel_sums(kind, source):
                for i, (lo, hi) in enumerate(((0, SEQ), (SEQ, T))):
                    out = open_bank((kind, i))
                    for c in range(CT):
                        last = mm(out[:, 0:hi - lo], ones_cw[:, :], source[:, c, lo:hi], start=c == 0, stop=c == CT - 1)
                    done(last)

            def ret_step(kind, t):
                name = (kind, t)
                r = ROWS[t]
                v_rows = z[0:r, t, S_V].rearrange("p (h d) -> p h d", h=HEADS)
                if kind == "ret_qT":
                    pe.wait_ge(s_rot, t + 1)
                    transposes(name, [q_rot[0:r, h, :] for h in range(HEADS)], r)
                elif kind == "ret_kT":
                    transposes(name, [k_rot[0:r, h, :] for h in range(HEADS)], r)
                elif kind == "ret_scores":
                    pe.wait_ge(s_by["dve"], EMPTIED[("ret_kT", t)])
                    out = open_bank(name)
                    for h in range(HEADS):
                        last = mm(out[0:r, h * P:h * P + r], kT[:, h, 0:r], qT[:, h, 0:r], start=True, stop=True)
                    done(last)
                elif kind == "ret_out":
                    pe.wait_ge(s_by["dve"], EMPTIED[("ret_scores", t)])
                    pe.wait_ge(s_by["act"], EMPTIED[("qkvg", S_V, t)])
                    if 0 < t < SAMPLE:
                        pe.wait_ge(s_by["dve"], EMPTIED[("ret_state", t - 1)])
                    if t == SAMPLE:
                        pe.wait_ge(s_st, 32)
                    out = open_bank(name)
                    for h in range(HEADS):
                        part = out[0:r, h * HD:(h + 1) * HD]
                        last = mm(part, sc_dec[0:r, h, 0:r], v_rows[:, h, :], start=True, stop=t == 0)
                        if t:
                            last = mm(part, qT_cross[t % 2][:, h, 0:r], state[:, 1 if t == SAMPLE else 0, h, :],
                                      start=False, stop=True)
                    done(last)
                elif kind == "ret_state":
                    pe.wait_ge(s_kdec, t + 1)
                    out = open_bank(name)
                    for h in range(HEADS):
                        last = mm(out[:, h * HD:(h + 1) * HD], k_dec[0:r, h, :], v_rows[:, h, :], start=True, stop=True)
                    done(last)
                else:
                    pe.wait_ge(s_on, t + 1)
                    transposes(name, [o_norm[0:r, h, :] for h in range(HEADS)], r)

            w = section(S_V)
            for name in retention_schedule():
                if name[0] == "qkvg":
                    t = name[2]
                    rows_times(name, hT, w, ROWS[t], t * P)
                    if t == SAMPLE:
                        pe.drain().then_inc(s_wsec, 1)
                elif name == ("ln_mean", 0):
                    pe.wait_ge(s_conv, 1)
                    channel_sums("ln_mean", conv)
                elif name == ("ln_var", 0):
                    pe.wait_ge(s_csq, CT)
                    channel_sums("ln_var", yT[:, HEADS:KD, :])
                elif name[0].startswith("ret_"):
                    ret_step(*name)
            pe.wait_ge(s_yconv, 1)
            pe.wait_ge(s_by["dve"], EMPTIED[("ret_yT", SAMPLE)])
            w_out = [section(S_OUT), section(S_OUT + 1)]
            for t in range(TILES):
                for i in range(2):
                    rows_times(("mix_out", t, i), yT, w_out[i], ROWS[t], t * P)
            pe.drain().then_inc(s_wsec, 2)
            row_transposes("ffn_t", TILES)
            pe.wait_ge(s_by["act"], EMPTIED[("ffn_t", SAMPLE, 1)])
            pe.wait_ge(s_keys, 16)
            for hs in range(SIDES + 1):
                if hs < SIDES:
                    if hs % 4 == 0:
                        w = section(S_QUERY + hs // 4)
                    cols = slice((hs % 4) * P, (hs % 4 + 1) * P)
                    for i, (lo, hi) in enumerate(((0, SEQ), (SEQ, T))):
                        out = open_bank(("query", hs, i))
                        for k in range(KD):
                            last = mm(out[:, 0:hi - lo], w[:, k, cols], hT[:, k, lo:hi], start=k == 0,
                                      stop=k == KD - 1)
                        done(last)
                    if hs % 4 == 3:
                        pe.drain().then_inc(s_wsec, 1)
                if hs:
                    side = hs - 1
                    head = side // 2
                    pe.wait_ge(s_by["act"], EMPTIED[("query", side, 1)])
                    out = open_bank(("scores", side))
                    j = head % FOLDED
                    mm(ps[j * DEC:(j + 1) * DEC, 7, (head // FOLDED * 2 + side % 2) * KEYS:][:, 0:KEYS],
                       queryT[:, side % 4, SEQ:T], keysT[:, side, :], start=True, stop=True)
                    for t in range(SAMPLE):
                        last = mm(out[:, t * KEYS:(t + 1) * KEYS], queryT[:, side % 4, t * P:(t + 1) * P],
                                  keysT[:, side, :], start=True, stop=True)
                    done(last)

            def sum_up(triple, m):
                vt = triple * 3 + m
                if not (isinstance(vt, int) and vt < 3):
                    pe.wait_ge(s_acc, vt - 2)
                    pe.nop(nofuse=True)
                for k in range(TOPK):
                    place = m * TOPK + k
                    slot = place % SLOTS
                    pe.wait_ge(s_slot[slot], triple * 64 + 16 * (place // SLOTS + 1))
                    pe.wait_ge(s_diag, vt * TOPK + k + 1)
                    for half in range(2):
                        last = mm(ps[:, 2 * m + half, :], diag[:, k % DIAGS, :],
                                  ring[:, slot, D + half * SEC:D + (half + 1) * SEC], start=k == 0, stop=k == TOPK - 1)
                    last.then_inc(s_used, 1)

            for m in range(3):
                sum_up(0, m)
            with pe.Fori(1, VT // 3) as triple:
                for m in range(3):
                    sum_up(triple, m)
            sum_up(VT // 3, 0)


_INS = ["x_prompt", "x_sample", "state_ret", "conv_state", "weights", "keys", "params", "consts", "gain_ffn",
        "gain_final", "experts"]
_OUTS = [("y_prompt", (SEQ, D)), ("y_sample", (DEC, D)), ("ret_prompt", (P, HEADS, HD)), ("ret_sample", (P, HEADS, HD)),
         ("conv_prompt", (P, CT, PAD)), ("conv_sample", (P, CT, PAD))]


def lay_out(inputs):
    a = {k: np.asarray(v) for k, v in inputs.items()}
    w_all = np.concatenate([a["w_in"][0], a["w_out"][0], a["peer_query"][0]], axis=1)
    weights = w_all.reshape(KD, P, SECTIONS, SEC).transpose(2, 1, 0, 3)

    def columns(x):
        return x.reshape(-1, P).T
    taps = a["conv_dw"][0].reshape(TAPS, CT, P).transpose(2, 1, 0).reshape(P, CT * TAPS)
    params = np.concatenate([columns(a["norm_mix"][0]), columns(a["ret_gn_gain"][0]), columns(a["conv_dw_bias"][0]),
                             columns(a["conv_ln_gain"][0]), columns(a["conv_ln_bias"][0]), taps], axis=1)
    out = {
        "x_prompt": a["x_prompt"][0], "x_sample": a["x_sample"][0],
        "state_ret": a["state_retention"][0, 0].transpose(1, 0, 2),
        "conv_state": a["state_conv"][0, 0].reshape(PAD, CT, P).transpose(2, 1, 0),
        "weights": weights,
        "keys": a["peer_sub_keys"][0].reshape(SIDES, KEYS, P).transpose(2, 0, 1),
        "params": params, "consts": shape_constants(),
        "gain_ffn": a["norm_ffn"], "gain_final": a["norm_final"][None, :],
        "experts": np.concatenate([a["peer_down"][0], a["peer_up"][0]], axis=1),
    }
    return {k: np.ascontiguousarray(v) for k, v in out.items()}


def program(nc, arrays):
    args = [nc.dram_tensor(n, arrays[n].shape, FP32, kind="ExternalInput").ap() for n in _INS]
    args += [nc.dram_tensor(n, shape, FP32, kind="ExternalOutput").ap() for n, shape in _OUTS]
    build(nc, *args)
    return nc


def kernel(**inputs):
    import concourse.bacc as bacc
    from concourse.bass_utils import run_bass_kernel_spmd
    arrays = lay_out(inputs)
    nc = program(bacc.Bacc("TRN2", target_bir_lowering=False, num_devices=1), arrays)
    r = run_bass_kernel_spmd(nc, [arrays], core_ids=[0]).results[0]
    ret = [r[n].transpose(1, 0, 2)[None, None] for n in ("ret_prompt", "ret_sample")]
    conv = [r[n].transpose(2, 1, 0).reshape(1, 1, PAD, CW) for n in ("conv_prompt", "conv_sample")]
    return (r["y_prompt"][None], r["y_sample"][None], ret[0], ret[1], conv[0], conv[1])
```

```python
import math
from contextlib import ExitStack

import numpy as np
import concourse.bass as bass
from concourse import mybir

FP32 = mybir.dt.float32
U32 = mybir.dt.uint32
ALU = mybir.AluOpType
ACT = mybir.ActivationFunctionType
AX = mybir.AxisListType

P = 128
D = 1024
KD = D // P
SEQ, DEC = 512, 32
T = SEQ + DEC
TILES = SEQ // P + 1
ROWS = [P] * (SEQ // P) + [DEC]
SAMPLE = TILES - 1
PAST = 256
HEADS, HD = 4, 128
RW = HEADS * HD
CW = D - RW
CT = CW // P
TAPS = 31
PAD = TAPS - 1
SEC = 512
SECTIONS = (4 * RW + 2 * CW + D) // SEC
S_Q, S_K, S_V, S_G, S_A, S_B, S_OUT = 0, 1, 2, 3, 4, 5, 6
WEIGHT_ORDER = [S_A, S_B, S_Q, S_K, S_G, S_V, S_OUT, S_OUT + 1]
WSLOTS = 3
PH, KEYS, TOPK = 8, 128, 16
EXPERTS = KEYS * KEYS
FOLDED = P // DEC
HT = TILES - 1
VT = HT * PH + PH // FOLDED
HEAD_W = KD * 2 * KEYS
EPS = 1e-6
LOWEST = -3.0e38
SLOTS = 8
GROUP = 4
GROUPS = TOPK // GROUP
DIAGS = 8
BUFS = HT
PROJ = 6


def shape_constants():
    f = np.float32
    half = HD // 2
    inv = (f(10000.0) ** (-np.arange(half, dtype=f) / f(half))).astype(f)
    pos = np.concatenate([np.arange(SEQ, dtype=f), f(PAST) + np.arange(DEC, dtype=f)])
    ang = (pos[:, None] * inv[None, :]).astype(f).astype(np.float64)
    trig = np.zeros((P, TILES, 2, half), f)
    for t in range(TILES):
        r = ROWS[t]
        trig[:r, t, 0] = np.cos(ang[t * P:t * P + r])
        trig[:r, t, 1] = np.sin(ang[t * P:t * P + r])
    log_gamma = np.log1p(-np.exp2(-5.0 - np.arange(HEADS)))
    i = np.arange(P)
    diff = i[None, :] - i[:, None]
    scale = HD ** -0.5
    decay = np.zeros((P, HEADS, P), f)
    cross = np.zeros((P, HEADS, P), f)
    key_decay = np.zeros((P, 2, HEADS), f)
    for h in range(HEADS):
        decay[:, h] = np.where(diff >= 0, np.exp(log_gamma[h] * np.maximum(diff, 0)), 0.0) * scale
        cross[:, h] = np.exp(log_gamma[h] * (i + 1.0))[None, :]
        key_decay[:, 0, h] = np.exp(log_gamma[h] * (P - 1.0 - i)) * scale
        key_decay[:DEC, 1, h] = np.exp(log_gamma[h] * (DEC - 1.0 - i[:DEC])) * scale
    ident = np.eye(P, dtype=f)
    fold = (np.arange(P)[:, None] % DEC == np.arange(P)[None, :]).astype(f)
    iota = np.broadcast_to(np.arange(TOPK, dtype=f), (P, TOPK))
    parts = [trig.reshape(P, -1), decay.reshape(P, -1), cross.reshape(P, -1), key_decay.reshape(P, -1),
             ident, fold, iota]
    return np.concatenate(parts, axis=1).astype(f)


C_TRIG = 0
C_DECAY = C_TRIG + TILES * HD
C_CROSS = C_DECAY + HEADS * P
C_KDEC = C_CROSS + HEADS * P
C_IDENT = C_KDEC + 2 * HEADS
C_FOLD = C_IDENT + P
C_IOTA = C_FOLD + P
C_WIDTH = C_IOTA + TOPK
G_MIX = 0
G_RET = G_MIX + KD
G_BIAS = G_RET + HEADS
G_LNG = G_BIAS + CT
G_LNB = G_LNG + CT
G_TAPS = G_LNB + CT
G_WIDTH = G_TAPS + CT * TAPS


def gammas(length):
    return [float(np.exp(np.log1p(-np.exp2(-5.0 - h)) * length)) for h in range(HEADS)]


def retention_schedule():
    def head(t):
        return [("ret_qT", t), ("ret_kT", t)] if t < TILES else []

    def out(t):
        return [("ret_out", t), ("ret_state", t)] if 0 <= t else []

    def scores(t):
        return [("ret_scores", t)] if t < TILES else []

    def back(t):
        return [("ret_yT", t)] if 0 <= t else []

    def mix(t, i):
        return [("mix_out", t, i)]
    v = [[("qkvg", S_V, t)] for t in range(TILES)]
    order = v[0] + [("ln_mean", 0), ("ln_mean", 1)] + head(0) + v[1] + [("ln_var", 0), ("ln_var", 1)] + scores(0)
    order += v[2]
    mid = {3: mix(0, 0), 4: mix(0, 1), 5: mix(1, 1)}
    end = {1: v[3], 2: v[4], 3: mix(1, 0)}
    for t in range(1, TILES + 1):
        order += head(t) + out(t - 1) + mid.get(t, []) + scores(t) + back(t - 1) + end.get(t, [])
    return order


def psum_jobs():
    jobs = [(("norm_t", t, i), "dve") for t in range(TILES) for i in range(2)]
    for s in (S_A, S_B):
        jobs += [(("glu", s, c), "act") for c in range(CT + 1)]
    for s in (S_Q, S_K, S_G):
        jobs += [(("qkvg", s, t), "act") for t in range(TILES)]
    jobs += [(name, "act" if name[0] == "qkvg" else "dve") for name in retention_schedule()]
    by = {"mix_out": "dve", "ffn_t": "act", "query": "act", "scores": "dve"}
    jobs += [(step, by[step[0]]) for step in TRANSITION if step[0] != "sum"]
    return jobs


def transition():
    def mix(t, i):
        return [("mix_out", t, i)]

    def turn(t):
        return [("ffn_t", t, 0), ("ffn_t", t, 1)]

    def query(t):
        return [("query", t)]

    def scores(t):
        return [("scores", t)]

    def sums(vt, g):
        return [("sum", vt, g)]
    order = mix(2, 0) + turn(0) + query(0) + mix(3, 0) + scores(0) + mix(4, 0) + turn(1) + query(1)
    order += mix(2, 1) + scores(1) + mix(3, 1) + mix(4, 1) + turn(2) + query(2) + sums(0, 0) + scores(2) + turn(3)
    order += sums(0, 1) + query(3) + sums(0, 2) + scores(3) + sums(0, 3) + turn(4)
    return order + sums(1, 0) + query(4) + sums(1, 1) + scores(4)


TRANSITION = transition()
JOBS = psum_jobs()
JOB = {name: n for n, (name, _) in enumerate(JOBS)}
EMPTIED = {}
_seen = {"dve": 0, "act": 0}
for _name, _by in JOBS:
    _seen[_by] += 1
    EMPTIED[_name] = _seen[_by]
BANKS = 7
FIRST_SUM = JOB[("ffn_t", 2, 0)]
Q_BANKS = 4
BANK = {name: n % BANKS if n < FIRST_SUM else Q_BANKS + (n - FIRST_SUM) % 3 for name, n in JOB.items()}
BEFORE = {}
_last = {}
for _name, _by in JOBS:
    if BANK[_name] in _last:
        BEFORE[_name] = _last[BANK[_name]]
    _last[BANK[_name]] = (_name, _by)


def build(nc, x_prompt, x_sample, state_ret, conv_state, weights, head_weights, params, consts, gain_ffn, gain_final,
          experts, y_prompt, y_sample, ret_prompt, ret_sample, conv_prompt, conv_sample):
    ctx = ExitStack()
    with ctx:
        def sb(name, shape, dt=FP32):
            return ctx.enter_context(nc.sbuf_tensor(name, shape, dt))

        def sem(name):
            return ctx.enter_context(nc.semaphore(name))

        z_at = WSLOTS * KD * SEC
        arena = sb("arena", [P, SLOTS * 2 * D + 2 * (HEAD_W + 2 * KEYS) + 2 * T + 2 * D])
        w_ring = arena[:, 0:z_at].rearrange("p (s k n) -> p s k n", s=WSLOTS, k=KD)
        z = arena[:, z_at:z_at + TILES * 4 * SEC].rearrange("p (t s n) -> p t s n", t=TILES, s=4)
        ring_rows = arena[:, 0:SLOTS * 2 * D].rearrange("p (s d) -> p s d", s=SLOTS)
        at = SLOTS * 2 * D
        head_w = []
        for i in range(2):
            head_w.append((arena[:, at:at + HEAD_W].rearrange("p (k n) -> p k n", k=KD),
                           arena[:, at + HEAD_W:at + HEAD_W + 2 * KEYS].rearrange("p (s n) -> p s n", s=2),
                           arena[:, at:at + HEAD_W + 2 * KEYS]))
            at += HEAD_W + 2 * KEYS
        queryT = arena[:, at:at + 2 * T].rearrange("p (s t) -> p s t", s=2)
        at += 2 * T
        product = arena[:, at:at + 2 * D].rearrange("p (b d) -> p b d", b=2)

        xs = sb("xs", [P, TILES, D])
        hn = sb("hn", [P, TILES, D])
        scratch = hn[:, :, :].rearrange("p t d -> p (t d)")

        def scratch4(n):
            return scratch[:, n * RW:(n + 1) * RW].rearrange("p (h d) -> p h d", h=HEADS)
        q_rot, k_rot, k_dec, qT, kT, sc_dec, o_norm = (scratch4(n) for n in range(7))
        qT_cross = [scratch4(7), scratch4(8)]
        hT = sb("hT", [P, KD, T])
        region_b = sb("region_b", [P, KD * T + CT * (SEQ + PAD + DEC + PAD) + CT * T])
        yT = region_b[:, 0:KD * T].rearrange("p (k t) -> p k t", k=KD)
        at = KD * T
        u_p = region_b[:, at:at + CT * (SEQ + PAD)].rearrange("p (c t) -> p c t", c=CT)
        conv_part = region_b[:, HEADS * T:KD * T]
        gate_tanh = conv_part[:, 0:2 * RW].rearrange("p (b n) -> p b n", b=2)
        deviation, newton = conv_part[:, 0:T], conv_part[:, T:2 * T]
        row_gain = region_b[:, at:at + D]
        scores = region_b[:, at + D:at + D + HT * 2 * KEYS].rearrange("p (t s n) -> p t s n", t=HT, s=2)
        at += CT * (SEQ + PAD)
        u_s = region_b[:, at:at + CT * (DEC + PAD)].rearrange("p (c t) -> p c t", c=CT)
        at += CT * (DEC + PAD)
        conv = region_b[:, at:at + CT * T].rearrange("p (c t) -> p c t", c=CT)
        diag = region_b[:, at:at + DIAGS * P].rearrange("p (k n) -> p k n", k=DIAGS)
        at += DIAGS * P
        sampleT = region_b[:, at:at + 2 * PH * DEC]

        cst = sb("cst", [P, C_WIDTH])
        par = sb("par", [P, G_WIDTH])
        half_ln = sb("half_ln", [P, 2 * CT])
        state = sb("state", [P, 2, HEADS, HD])
        ones_cw = sb("ones_cw", [P, P])
        neg_half = sb("neg_half", [P, 1])
        sq_sum = sb("sq_sum", [P, 3 * TILES])
        rstd = sb("rstd", [P, 3 * TILES])
        bn = sb("bn", [P, HEADS, 6])
        mv = sb("mv", [P, HEADS, 2])
        ret_rstd = sb("ret_rstd", [P, HEADS])
        var = sb("var", [P, T])
        rot_tmp = sb("rot_tmp", [P, HEADS, HD // 2])

        flat_state = state[:, :, :, :].rearrange("p w h d -> p (w h d)")
        cand = flat_state[:, 2 * KEYS:2 * KEYS + TOPK * TOPK]
        cand_cut = flat_state[:, 2 * KEYS + TOPK * TOPK:2 * KEYS + 2 * TOPK * TOPK]
        picks = cst[:, C_TRIG:C_TRIG + 2 * TOPK * TOPK].rearrange("p (s a b) -> p s a b", s=2, a=TOPK)

        trig = cst[:, C_TRIG:C_DECAY].rearrange("p (t c n) -> p t c n", t=TILES, c=2)
        decay = cst[:, C_DECAY:C_CROSS].rearrange("p (h n) -> p h n", h=HEADS)
        cross = cst[:, C_CROSS:C_KDEC].rearrange("p (h n) -> p h n", h=HEADS)
        key_decay = cst[:, C_KDEC:C_IDENT].rearrange("p (c h) -> p c h", c=2)
        ident = cst[:, C_IDENT:C_FOLD]
        fold = cst[:, C_FOLD:C_IOTA]
        iota = cst[:, C_IOTA:C_WIDTH]

        sc_cut = var[:, 0:2 * KEYS].rearrange("p (s n) -> p s n", s=2)
        top_s = sb("top_s", [P, 2, TOPK])
        top_i = sb("top_i", [P, 2, TOPK], U32)
        top_f = sb("top_f", [P, 2, TOPK])
        best_s = sb("best_s", [P, TOPK])
        best_i = sb("best_i", [P, TOPK], U32)
        pair_i = sb("pair_i", [P, 2, TOPK], U32)
        pair_f = sb("pair_f", [P, 2, TOPK])
        picked = sb("picked", [P, 2, TOPK])
        expert_f = sb("expert_f", [P, TOPK])
        expert = sb("expert", [P, BUFS, TOPK], U32)
        neg_max = sb("neg_max", [P, BUFS])
        best_kept = sb("best_kept", [P, BUFS, TOPK])
        gate = sb("gate", [P, BUFS, TOPK])
        gate_sum = sb("gate_sum", [P, BUFS])
        dots = sb("dots", [P, TOPK])
        gl = sb("gl", [P, 3, GROUP])
        gl_tanh = sb("gl_tanh", [P, GROUP])
        weight = sb("weight", [P, 2, GROUP])

        ps = ctx.enter_context(nc.psum_tensor("ps", [P, 8, SEC], FP32))

        def bank(name):
            return ps[:, BANK[name], :]

        def rows_of(slot):
            return ring_rows[:, (slot + SLOTS // 2) % SLOTS]

        s_x = [sem(f"s_x{t}") for t in range(TILES)]
        s_ident = sem("s_ident")
        s_cst = sem("s_cst")
        s_par = sem("s_par")
        s_w = [sem(f"s_w{i}") for i in range(WSLOTS)]
        s_hw = [sem("s_hw_first"), sem("s_hw_later")]
        s_gain = sem("s_gain")
        s_gain2 = sem("s_gain2")
        s_st = sem("s_st")
        s_pe = sem("s_pe")
        s_by = {"dve": sem("s_by_dve"), "act": sem("s_by_act")}
        s_setup = sem("s_setup")
        s_sq = sem("s_sq")
        s_mean = sem("s_mean")
        s_rstd = sem("s_rstd")
        s_hn = sem("s_hn")
        s_wsec = sem("s_wsec")
        s_u = sem("s_u")
        s_conv = sem("s_conv")
        s_convout = sem("s_convout")
        s_gt = sem("s_gt")
        s_gate = sem("s_gate")
        s_csq = sem("s_csq")
        s_dev = sem("s_dev")
        s_yh = sem("s_yh")
        s_yt = sem("s_yt")
        s_yconv = sem("s_yconv")
        s_rot = sem("s_rot")
        s_kdec = sem("s_kdec")
        s_retout = sem("s_retout")
        s_ostat = sem("s_ostat")
        s_orstd = sem("s_orstd")
        s_on = sem("s_on")
        s_rep = sem("s_rep")
        s_proj = sem("s_proj")
        s_queries = sem("s_queries")
        s_scored = sem("s_scored")
        s_turned = sem("s_turned")
        s_out = sem("s_out")
        s_idx = sem("s_idx")
        s_exp = sem("s_exp")
        s_slot = [sem(f"s_slot{i}") for i in range(SLOTS)]
        s_used = sem("s_used")
        s_poly = sem("s_poly")
        s_tanh = sem("s_tanh")
        s_wt = sem("s_wt")
        s_diag = sem("s_diag")
        s_acc = sem("s_acc")
        s_yout = sem("s_yout")

        def slot_filled(vt, k):
            return vt * (TOPK // SLOTS * 16) + 16 * (k // SLOTS + 1)

        block = ctx.enter_context(nc.Block())

        @block.sync
        def _(sp):
            for t in range(TILES):
                rows = x_prompt[t * P:(t + 1) * P, :] if t < SAMPLE else x_sample
                sp.dma_start(xs[0:ROWS[t], t, :], rows).then_inc(s_x[t], 16)
            sp.dma_start(cst[:, C_IDENT:], consts[:, C_IDENT:]).then_inc(s_ident, 16)
            sp.dma_start(par[:, :], params).then_inc(s_par, 16)
            for n, s in enumerate(WEIGHT_ORDER):
                if n >= WSLOTS:
                    sp.wait_ge(s_wsec, n - WSLOTS + 1)
                sp.dma_start(w_ring[:, n % WSLOTS], weights[s]).then_inc(s_w[n % WSLOTS], 16)
                if n == 0:
                    sp.dma_start(cst[:, 0:C_IDENT], consts[:, 0:C_IDENT]).then_inc(s_cst, 16)
                    sp.dma_start(u_s[:, :, 0:PAD], conv_state).then_inc(s_st, 16)
                    sp.dma_start(state[:, 1], state_ret).then_inc(s_st, 16)
                if WEIGHT_ORDER[n] == S_OUT + 1:
                    sp.wait_ge(s_u, 1)
                    sp.dma_start(conv_prompt, u_p[:, :, SEQ:SEQ + PAD]).then_inc(s_convout, 16)
                    sp.dma_start(conv_sample, u_s[:, :, DEC:DEC + PAD]).then_inc(s_convout, 16)
                    sp.wait_ge(s_convout, 32)
                    sp.wait_ge(s_conv, 1)
                    sp.dma_start(row_gain, gain_ffn.to_broadcast([P, D])).then_inc(s_gain, 16)
            sp.wait_ge(s_by["dve"], EMPTIED[("ret_yT", SAMPLE)])
            sp.dma_start(head_w[0][2], head_weights[0]).then_inc(s_hw[0], 16)
            sp.dma_start(head_w[1][2], head_weights[1]).then_inc(s_hw[1], 16)
            sp.dma_start(ret_prompt, state[:, 0]).then_inc(s_retout, 16)
            sp.dma_start(ret_sample, state[:, 1]).then_inc(s_retout, 16)
            sp.wait_ge(s_hn, 2 * TILES)
            for j in range(1, FOLDED):
                sp.dma_start(hn[j * DEC:(j + 1) * DEC, SAMPLE, :], hn[0:DEC, SAMPLE, :]).then_inc(s_rep, 16)
            sp.dma_start(row_gain, gain_final.to_broadcast([P, D])).then_inc(s_gain2, 16)
            for head in range(2, PH):
                sp.wait_ge(s_proj, (head - 1) * PROJ)
                sp.dma_start(head_w[1][2], head_weights[head]).then_inc(s_hw[1], 16)
            for t in range(TILES):
                sp.wait_ge(s_yout, t + 1)
                out = y_prompt[t * P:(t + 1) * P, :] if t < SAMPLE else y_sample
                sp.dma_start(out, xs[0:ROWS[t], t, :]).then_inc(s_out, 16)
            sp.wait_ge(s_out, 16 * TILES)
            sp.wait_ge(s_convout, 32)
            sp.wait_ge(s_retout, 32)

        @block.gpsimd
        def _(pool):
            nc.gpsimd.memset(neg_half[:, :], -0.5)
            pool.drain()

            means = []

            def inverse_root(out, in_, rows, n, ready):
                nc.gpsimd.tensor_scalar(out=out, in0=in_, scalar1=1.0 / n, scalar2=EPS, op0=ALU.mult, op1=ALU.add)\
                    .then_inc(s_mean, 1)
                means.append(out)
                pool.wait_ge(s_mean, len(means))
                width = out.shape[-1]
                power = neg_half[0:rows, 0:1]
                nc.gpsimd.tensor_tensor(out=out, in0=out, in1=power if width == 1 else power.to_broadcast([rows, width]),
                                        op=ALU.pow).then_inc(ready, 1)

            for t in range(TILES):
                pool.wait_ge(s_sq, t + 1)
                inverse_root(rstd[0:ROWS[t], t:t + 1], sq_sum[0:ROWS[t], t:t + 1], ROWS[t], D, s_rstd)

            half = HD // 2
            pool.wait_ge(s_cst, 16)

            def retention_root(t):
                pool.wait_ge(s_ostat, t + 1)
                inverse_root(ret_rstd[0:ROWS[t], :], mv[0:ROWS[t], :, 1], ROWS[t], 1, s_orstd)

            for t in range(TILES):
                r = ROWS[t]
                pool.wait_ge(s_by["act"], EMPTIED[("qkvg", S_K, t)])
                if t:
                    pool.wait_ge(s_pe, JOB[("ret_kT", t - 1)] + 1)
                cos = trig[0:r, t, 0].unsqueeze(1).to_broadcast([r, HEADS, half])
                sin = trig[0:r, t, 1].unsqueeze(1).to_broadcast([r, HEADS, half])
                tmp = rot_tmp[0:r]
                for col, dst in ((0, q_rot), (1, k_rot)):
                    src = z[0:r, t, col].rearrange("p (h d) -> p h d", h=HEADS)
                    x1, x2 = src[:, :, 0:half], src[:, :, half:HD]
                    for a, b, o, op in ((x1, x2, dst[0:r, :, 0:half], ALU.subtract),
                                        (x2, x1, dst[0:r, :, half:HD], ALU.add)):
                        nc.gpsimd.tensor_tensor(out=o, in0=a, in1=cos, op=ALU.mult)
                        nc.gpsimd.tensor_tensor(out=tmp, in0=b, in1=sin, op=ALU.mult)
                        pool.drain()
                        nc.gpsimd.tensor_tensor(out=o, in0=o, in1=tmp, op=op)
                        pool.drain()
                pool.drain().then_inc(s_rot, 1)
                if t:
                    retention_root(t - 1)
                    pool.wait_ge(s_pe, JOB[("ret_state", t - 1)] + 1)
                kd = key_decay[0:r, 1 if t == SAMPLE else 0].unsqueeze(2).to_broadcast([r, HEADS, HD])
                nc.gpsimd.tensor_tensor(out=k_dec[0:r], in0=k_rot[0:r], in1=kd, op=ALU.mult).then_inc(s_kdec, 1)
            retention_root(SAMPLE)

            def mixed_root(t):
                pool.wait_ge(s_sq, TILES + t + 1)
                c = TILES + t
                inverse_root(rstd[0:ROWS[t], c:c + 1], sq_sum[0:ROWS[t], c:c + 1], ROWS[t], D, s_rstd)

            def gathers(vt, m, lo=0, hi=TOPK):
                if lo == 0:
                    pool.wait_ge(s_idx, vt + 1)
                    pool.nop(nofuse=True)
                for k in range(lo, hi):
                    if not (isinstance(vt, int) and vt == 0 and k < SLOTS):
                        pool.wait_ge(s_used, vt * TOPK + (k - SLOTS + 1))
                        pool.nop(nofuse=True)
                    pool.indirect_dma_start(rows_of(k % SLOTS), None, experts,
                                            bass.IndirectOffsetOnAxis(ap=expert[:, m, k:k + 1], axis=0))\
                        .then_inc(s_slot[k % SLOTS], 16)

            def final_root(t):
                pool.wait_ge(s_sq, 2 * TILES + t + 1)
                c = 2 * TILES + t
                inverse_root(rstd[0:ROWS[t], c:c + 1], sq_sum[0:ROWS[t], c:c + 1], ROWS[t], D, s_rstd)

            mixed_root(0)
            mixed_root(1)
            gathers(0, 0, 0, SLOTS // 2)
            pool.wait_ge(s_wsec, len(WEIGHT_ORDER) - 1)
            gathers(0, 0, SLOTS // 2, SLOTS // 2 + 2)
            for t in range(2, SAMPLE):
                mixed_root(t)
            pool.wait_ge(s_wsec, len(WEIGHT_ORDER))
            gathers(0, 0, SLOTS // 2 + 2, SLOTS)
            mixed_root(SAMPLE)
            gathers(0, 0, SLOTS, TOPK)
            for m in range(1, HT):
                gathers(m, m)
            with pool.Fori(1, PH) as head:
                for m in range(HT):
                    gathers(head * HT + m, m)
            for vt in range(PH * HT, VT):
                gathers(vt, vt % BUFS)
            for t in range(TILES):
                final_root(t)

        @block.scalar
        def _(act):
            def square_sum(src, col, rows, junk):
                nc.scalar.activation(junk, src, ACT.Square, accum_out=sq_sum[0:rows, col:col + 1]).then_inc(s_sq, 1)

            def emptied(ins):
                ins.then_inc(s_by["act"], 1)

            def filled(name):
                act.wait_ge(s_pe, JOB[name] + 1)

            for t in range(TILES):
                act.wait_ge(s_x[t], 16)
                square_sum(xs[0:ROWS[t], t], t, ROWS[t], hn[0:ROWS[t], t])
            for s in (S_A, S_B):
                func, scale = (ACT.Copy, 0.5) if s == S_A else (ACT.Tanh, 0.5)
                for c in range(CT + 1):
                    filled(("glu", s, c))
                    src = bank(("glu", s, c))
                    if c < CT:
                        dst = u_p[:, c, PAD:PAD + SEQ] if s == S_A else conv[:, c, 0:SEQ]
                    else:
                        src = src[:, 0:CT * DEC].rearrange("p (c t) -> p c t", c=CT)
                        dst = u_s[:, :, PAD:PAD + DEC] if s == S_A else conv[:, :, SEQ:T]
                    emptied(nc.scalar.activation(dst, src, func, scale=scale))

            def rows_in(s, t):
                r = ROWS[t]
                filled(("qkvg", s, t))
                src = bank(("qkvg", s, t))[0:r]
                if s == S_G:
                    if t >= 2:
                        act.wait_ge(s_gate, t - 1)
                    nc.scalar.activation(gate_tanh[0:r, t % 2], src, ACT.Tanh, scale=0.5)
                    emptied(nc.scalar.activation(z[0:r, t, s], src, ACT.Copy, scale=0.5))
                else:
                    emptied(nc.scalar.activation(z[0:r, t, s], src, ACT.Copy))

            for s in (S_Q, S_K, S_G):
                for t in range(TILES):
                    rows_in(s, t)
            rows_in(S_V, 0)
            act.wait_ge(s_by["dve"], EMPTIED[("ln_mean", 1)])
            for c in range(CT):
                nc.scalar.activation(yT[:, HEADS + c, :], conv[:, c, :], ACT.Square).then_inc(s_csq, 1)
            rows_in(S_V, 1)
            act.wait_ge(s_by["dve"], EMPTIED[("ln_var", 1)])
            nc.scalar.activation(deviation, var[:, :], ACT.Sqrt).then_inc(s_dev, 1)
            rows_in(S_V, 2)
            act.wait_ge(s_yh, 1)
            for c in range(CT):
                nc.scalar.activation(yT[:, HEADS + c, :], conv[:, c, :], ACT.Tanh).then_inc(s_yt, 1)
            rows_in(S_V, 3)
            rows_in(S_V, 4)

            def mixed_squares(t):
                act.wait_ge(s_by["dve"], EMPTIED[("ret_yT", SAMPLE)])
                act.wait_ge(s_by["dve"], EMPTIED[("mix_out", t, 1)])
                square_sum(xs[0:ROWS[t], t], TILES + t, ROWS[t], hn[0:ROWS[t], t])

            def turned_rows(t):
                r = ROWS[t]
                for i in range(2):
                    name = ("ffn_t", t, i)
                    filled(name)
                    src = bank(name).rearrange("p (k t) -> p k t", k=4)[:, :, 0:r]
                    emptied(nc.scalar.activation(hT[:, 4 * i:4 * i + 4, t * P:t * P + r], src, ACT.Copy))

            def first_query(t):
                r = ROWS[t]
                filled(("query", t))
                src = bank(("query", t))[:, 0:2 * P].rearrange("p (s t) -> p s t", s=2)[:, :, 0:r]
                emptied(nc.scalar.activation(queryT[:, :, t * P:t * P + r], src, ACT.Copy))

            def later_query(head, i):
                act.wait_ge(s_proj, (head - 1) * PROJ + (i + 1))
                act.nop(nofuse=True)
                if i < 2:
                    dst, src = queryT[:, i, 0:SEQ], ps[:, Q_BANKS + i, :]
                else:
                    dst = queryT[:, :, SEQ:T]
                    src = ps[:, Q_BANKS + 2, 0:2 * DEC].rearrange("p (s t) -> p s t", s=2)
                nc.scalar.activation(dst, src, ACT.Copy).then_inc(s_queries, 1)

            def head_tile(vt, m, base, behind={}):
                act.wait_ge(s_idx, vt + 1)
                act.nop(nofuse=True)
                nc.scalar.activation(gate[:, m, :], best_kept[:, m, :], ACT.Exp, bias=neg_max[:, m:m + 1],
                                     accum_out=gate_sum[:, m:m + 1]).then_inc(s_exp, 1)
                for g in range(GROUPS):
                    group = vt * GROUPS + g
                    act.wait_ge(s_poly, group + 1)
                    nc.scalar.activation(gl_tanh[:, :], gl[:, 2, :], ACT.Tanh, scale=math.sqrt(2.0 / math.pi))\
                        .then_inc(s_tanh, 1)
                    act.wait_ge(s_wt, group + 1)
                    act.nop(nofuse=True)
                    for i in range(GROUP):
                        k = g * GROUP + i
                        if not (isinstance(vt, int) and vt == 0 and k < DIAGS):
                            act.wait_ge(s_used, vt * TOPK + (k - DIAGS + 1))
                        nc.scalar.activation(diag[:, k % DIAGS, :], base, ACT.Copy, scale=weight[:, g % 2, i:i + 1])\
                            .then_inc(s_diag, 1)
                    if g in behind:
                        behind[g]()

            def prompt_head(head, last=False):
                first = {2: lambda: later_query(head + 1, 0)}
                second = {0: lambda: later_query(head + 1, 1), 2: lambda: later_query(head + 1, 2)}
                behind = [{}, {}] if last else [first, second]
                for m in range(HT):
                    head_tile(head * HT + m, m, ident, behind[m] if m < 2 else {})

            for t in range(2):
                mixed_squares(t)
                turned_rows(t)
                first_query(t)
            mixed_squares(2)
            mixed_squares(3)

            def behind_first():
                turned_rows(2)
                first_query(2)
                mixed_squares(SAMPLE)
            head_tile(0, 0, ident, {0: behind_first, 1: lambda: turned_rows(3), 2: lambda: first_query(3)})
            head_tile(1, 1, ident, {0: lambda: turned_rows(4), 1: lambda: first_query(4),
                                    2: lambda: later_query(1, 0), 3: lambda: later_query(1, 1)})
            head_tile(2, 2, ident, {0: lambda: later_query(1, 2)})
            head_tile(3, 3, ident)
            with act.Fori(1, PH - 1) as head:
                prompt_head(head)
            prompt_head(PH - 1, last=True)
            head_tile(VT - 2, (VT - 2) % BUFS, fold)
            act.wait_ge(s_acc, VT - 2)
            for t in range(SAMPLE):
                square_sum(xs[0:ROWS[t], t], 2 * TILES + t, ROWS[t], hn[0:ROWS[t], t])
            head_tile(VT - 1, (VT - 1) % BUFS, fold)
            act.wait_ge(s_acc, VT)
            square_sum(xs[0:DEC, SAMPLE], 2 * TILES + SAMPLE, DEC, hn[0:DEC, SAMPLE])

        @block.vector
        def _(dve):
            v = nc.vector

            def emptied(ins):
                ins.then_inc(s_by["dve"], 1)

            def filled(name):
                dve.wait_ge(s_pe, JOB[name] + 1)

            v.memset(ones_cw[:, :], 1.0 / CW)
            v.memset(u_p[:, :, 0:PAD], 0.0).then_inc(s_setup, 1)
            for t in range(TILES):
                r = ROWS[t]
                dve.wait_ge(s_rstd, t + 1)
                v.tensor_scalar(out=hn[0:r, t], in0=xs[0:r, t], scalar1=rstd[0:r, t:t + 1], scalar2=None,
                                op0=ALU.mult).then_inc(s_hn, 1)
            dve.wait_ge(s_par, 16)
            v.tensor_scalar(out=half_ln[:, :], in0=par[:, G_LNG:G_TAPS], scalar1=0.5, scalar2=None, op0=ALU.mult)
            for t in range(TILES):
                r = ROWS[t]
                for i in range(2):
                    name = ("norm_t", t, i)
                    filled(name)
                    src = bank(name).rearrange("p (k t) -> p k t", k=4)[:, :, 0:r]
                    gain = par[:, G_MIX + 4 * i:G_MIX + 4 * i + 4].unsqueeze(2).to_broadcast([P, 4, r])
                    emptied(v.tensor_tensor(out=hT[:, 4 * i:4 * i + 4, t * P:t * P + r], in0=src, in1=gain,
                                            op=ALU.mult))
            dve.wait_ge(s_by["act"], EMPTIED[("glu", S_B, CT)])
            dve.wait_ge(s_st, 32)
            for c in range(CT):
                v.scalar_tensor_tensor(out=u_p[:, c, PAD:PAD + SEQ], in0=conv[:, c, 0:SEQ], scalar=1.0,
                                       in1=u_p[:, c, PAD:PAD + SEQ], op0=ALU.add, op1=ALU.mult)
            v.scalar_tensor_tensor(out=u_s[:, :, PAD:PAD + DEC], in0=conv[:, :, SEQ:T], scalar=1.0,
                                   in1=u_s[:, :, PAD:PAD + DEC], op0=ALU.add, op1=ALU.mult).then_inc(s_u, 1)
            dve.drain()
            for j in range(TAPS):
                for c in range(CT):
                    tap = par[:, G_TAPS + c * TAPS + j:G_TAPS + c * TAPS + j + 1]
                    for src, lo, n in ((u_p, 0, SEQ), (u_s, SEQ, DEC)):
                        out = conv[:, c, lo:lo + n]
                        if j == 0:
                            v.tensor_scalar(out=out, in0=src[:, c, 0:n], scalar1=tap,
                                            scalar2=par[:, G_BIAS + c:G_BIAS + c + 1], op0=ALU.mult, op1=ALU.add)
                        else:
                            last = v.scalar_tensor_tensor(out=out, in0=src[:, c, j:j + n], scalar=tap, in1=out,
                                                          op0=ALU.mult, op1=ALU.add)
                if j < TAPS - 1:
                    dve.drain()
            last.then_inc(s_conv, 1)
            for t in range(TILES):
                r = ROWS[t]
                dve.wait_ge(s_by["act"], EMPTIED[("qkvg", S_G, t)])
                v.scalar_tensor_tensor(out=z[0:r, t, S_G], in0=gate_tanh[0:r, t % 2], scalar=1.0, in1=z[0:r, t, S_G],
                                       op0=ALU.add, op1=ALU.mult).then_inc(s_gate, 1)
            def mean_off():
                for i, (lo, hi) in enumerate(((0, SEQ), (SEQ, T))):
                    filled(("ln_mean", i))
                    mean = bank(("ln_mean", i))[:, 0:hi - lo].unsqueeze(1).to_broadcast([P, CT, hi - lo])
                    emptied(v.tensor_tensor(out=conv[:, :, lo:hi], in0=conv[:, :, lo:hi], in1=mean, op=ALU.subtract))

            def variance():
                for i, (lo, hi) in enumerate(((0, SEQ), (SEQ, T))):
                    filled(("ln_var", i))
                    emptied(v.tensor_scalar(out=var[:, lo:hi], in0=bank(("ln_var", i))[:, 0:hi - lo], scalar1=EPS,
                                            scalar2=None, op0=ALU.add))

            def conv_norm():
                dve.wait_ge(s_dev, 1)
                v.reciprocal(deviation, deviation)
                dve.drain()
                v.tensor_tensor(out=newton, in0=deviation, in1=deviation, op=ALU.mult)
                dve.drain()
                v.tensor_tensor(out=newton, in0=newton, in1=var[:, :], op=ALU.mult)
                dve.drain()
                v.tensor_scalar(out=newton, in0=newton, scalar1=-0.5, scalar2=1.5, op0=ALU.mult, op1=ALU.add)
                dve.drain()
                v.tensor_tensor(out=var[:, :], in0=newton, in1=deviation, op=ALU.mult)
                dve.drain()
                v.tensor_tensor(out=conv[:, :, :], in0=conv[:, :, :],
                                in1=var[:, :].unsqueeze(1).to_broadcast([P, CT, T]), op=ALU.mult)
                dve.drain()
                for c in range(CT):
                    last = v.tensor_scalar(out=conv[:, c, :], in0=conv[:, c, :], scalar1=half_ln[:, c:c + 1],
                                           scalar2=half_ln[:, CT + c:CT + c + 1], op0=ALU.mult, op1=ALU.add)
                last.then_inc(s_yh, 1)

            def conv_silu():
                dve.wait_ge(s_yt, CT)
                v.scalar_tensor_tensor(out=yT[:, HEADS:KD, :], in0=yT[:, HEADS:KD, :], scalar=1.0, in1=conv[:, :, :],
                                       op0=ALU.add, op1=ALU.mult).then_inc(s_yconv, 1)

            def four(name, n):
                return bank(name).rearrange("p (h n) -> p h n", h=HEADS)[:, :, 0:n]

            def ret_step(kind, t):
                name = (kind, t)
                r = ROWS[t]
                filled(name)
                if kind == "ret_qT":
                    v.tensor_copy(qT[:, :, 0:r], four(name, r))
                    emptied(v.tensor_tensor(out=qT_cross[t % 2][:, :, 0:r], in0=four(name, r), in1=cross[:, :, 0:r],
                                            op=ALU.mult))
                elif kind == "ret_kT":
                    emptied(v.tensor_copy(kT[:, :, 0:r], four(name, r)))
                elif kind == "ret_scores":
                    emptied(v.tensor_tensor(out=sc_dec[0:r, :, 0:r], in0=four(name, r)[0:r], in1=decay[0:r, :, 0:r],
                                            op=ALU.mult))
                elif kind == "ret_out":
                    o = four(name, HD)[0:r]
                    for h in range(HEADS):
                        v.bn_stats(bn[0:r, h, :], o[:, h, :])
                    dve.drain()
                    for h in range(HEADS):
                        last = v.bn_aggr(mv[0:r, h, :], bn[0:r, h, :])
                    last.then_inc(s_ostat, 1)
                    dve.wait_ge(s_orstd, t + 1)
                    for h in range(HEADS):
                        last = v.tensor_scalar(out=o_norm[0:r, h, :], in0=o[:, h, :], scalar1=mv[0:r, h, 0:1],
                                               scalar2=ret_rstd[0:r, h:h + 1], op0=ALU.subtract, op1=ALU.mult)
                    emptied(last)
                    dve.drain()
                    v.tensor_tensor(out=o_norm[0:r], in0=o_norm[0:r],
                                    in1=z[0:r, t, S_G].rearrange("p (h d) -> p h d", h=HEADS), op=ALU.mult)\
                        .then_inc(s_on, 1)
                elif kind == "ret_state":
                    add = four(name, HD)
                    which, length = (1, DEC) if t == SAMPLE else (0, P)
                    if t == 0:
                        last = v.tensor_copy(state[:, 0], add)
                    else:
                        for h, g in enumerate(gammas(length)):
                            last = v.scalar_tensor_tensor(out=state[:, which, h], in0=state[:, which, h], scalar=g,
                                                          in1=add[:, h], op0=ALU.mult, op1=ALU.add)
                    emptied(last)
                else:
                    gain = par[:, G_RET:G_RET + HEADS].unsqueeze(2).to_broadcast([P, HEADS, r])
                    emptied(v.tensor_tensor(out=yT[:, 0:HEADS, t * P:t * P + r], in0=four(name, r), in1=gain,
                                            op=ALU.mult))

            def mix_add(t, i):
                name = ("mix_out", t, i)
                filled(name)
                part = xs[0:ROWS[t], t, i * SEC:(i + 1) * SEC]
                emptied(v.tensor_tensor(out=part, in0=bank(name)[0:ROWS[t]], in1=part, op=ALU.add))

            dve.wait_ge(s_cst, 16)
            for name in retention_schedule():
                if name == ("ln_mean", 0):
                    mean_off()
                elif name[0] == "mix_out":
                    mix_add(*name[1:])
                elif name == ("ln_var", 0):
                    variance()
                elif name[0].startswith("ret_"):
                    ret_step(*name)
                    if name == ("ret_scores", 0):
                        conv_norm()
                    elif name == ("ret_yT", 0):
                        conv_silu()
            def peer_norm(t):
                r = ROWS[t]
                dve.wait_ge(s_rstd, TILES + t + 1)
                v.scalar_tensor_tensor(out=hn[0:r, t], in0=xs[0:r, t], scalar=rstd[0:r, TILES + t:TILES + t + 1],
                                       in1=row_gain[0:r, :], op0=ALU.mult, op1=ALU.mult).then_inc(s_hn, 1)

            def first_scores(t):
                name = ("scores", t)
                filled(name)
                if t < SAMPLE:
                    src = bank(name)[:, 0:2 * KEYS].rearrange("p (s n) -> p s n", s=2)
                    emptied(v.tensor_copy(scores[:, t], src))
                else:
                    src = bank(name)[:, 0:2 * DEC].rearrange("p (s n) -> p s n", s=2)
                    dst = sampleT.rearrange("p (s n) -> p s n", s=2)[:, :, 0:DEC]
                    emptied(v.tensor_copy(dst, src))
                dve.drain()

            def later_scores(head):
                for s in range(2):
                    dve.wait_ge(s_proj, (head - 1) * PROJ + (4 + s))
                    dve.nop(nofuse=True)
                    src = ps[:, Q_BANKS + s, :].rearrange("p (t n) -> p t n", t=HT)
                    v.tensor_copy(scores[:, :, s, :], src).then_inc(s_scored, 1)
                dve.wait_ge(s_proj, head * PROJ)
                dve.nop(nofuse=True)
                for s in range(2):
                    last = v.tensor_copy(sampleT[:, bass.ds(head * DEC + s * PH * DEC, DEC)],
                                         ps[:, Q_BANKS + 2, s * DEC:(s + 1) * DEC])
                last.then_inc(s_scored, 1)
                dve.drain()

            def top16(values, cut, best, index):
                v.max(best[:, 0:8], values)
                dve.drain()
                v.max_index(index[:, 0:8], best[:, 0:8], values)
                v.match_replace(cut, best[:, 0:8], values, LOWEST)
                dve.drain()
                v.max(best[:, 8:16], cut)
                dve.drain()
                v.max_index(index[:, 8:16], best[:, 8:16], cut)

            def choose(place, u, between=()):
                between = list(between)

                def pause():
                    if between:
                        between.pop(0)()
                top16(scores[:, place, 0, :], sc_cut[:, 0, :], top_s[:, 0, :], top_i[:, 0, :])
                pause()
                top16(scores[:, place, 1, :], sc_cut[:, 1, :], top_s[:, 1, :], top_i[:, 1, :])
                dve.drain()
                v.tensor_copy(top_f[:, :, :], top_i[:, :, :])
                v.tensor_tensor(out=cand[:, :].rearrange("p (a b) -> p a b", a=TOPK),
                                in0=top_s[:, 0, :].unsqueeze(2).to_broadcast([P, TOPK, TOPK]),
                                in1=top_s[:, 1, :].unsqueeze(1).to_broadcast([P, TOPK, TOPK]), op=ALU.add)
                dve.drain()
                pause()
                top16(cand[:, :], cand_cut[:, :], best_s[:, :], best_i[:, :])
                dve.drain()
                pause()
                v.tensor_copy(best_kept[:, u, :], best_s[:, :])
                v.tensor_scalar(out=neg_max[:, u:u + 1], in0=best_s[:, 0:1], scalar1=-1.0, scalar2=None, op0=ALU.mult)
                v.tensor_scalar(out=pair_i[:, 0, :], in0=best_i[:, :], scalar1=4, scalar2=None,
                                op0=ALU.logical_shift_right)
                v.tensor_scalar(out=pair_i[:, 1, :], in0=best_i[:, :], scalar1=TOPK - 1, scalar2=None,
                                op0=ALU.bitwise_and)
                dve.drain()
                v.tensor_copy(pair_f[:, :, :], pair_i[:, :, :])
                dve.drain()
                for s in range(2):
                    v.tensor_tensor(out=picks[:, s], in0=pair_f[:, s, :].unsqueeze(2).to_broadcast([P, TOPK, TOPK]),
                                    in1=iota.unsqueeze(1).to_broadcast([P, TOPK, TOPK]), op=ALU.is_equal)
                dve.drain()
                for s in range(2):
                    v.tensor_tensor(out=picks[:, s], in0=picks[:, s],
                                    in1=top_f[:, s, :].unsqueeze(1).to_broadcast([P, TOPK, TOPK]), op=ALU.mult)
                dve.drain()
                v.tensor_reduce(out=picked[:, :, :], in_=picks[:, :, :, :], axis=AX.X, op=ALU.add)
                dve.drain()
                v.scalar_tensor_tensor(out=expert_f[:, :], in0=picked[:, 0, :], scalar=float(KEYS), in1=picked[:, 1, :],
                                       op0=ALU.mult, op1=ALU.add)
                dve.drain()
                v.tensor_copy(expert[:, u, :], expert_f[:, :]).then_inc(s_idx, 1)
                for rest in between:
                    rest()

            def soft(vt, m):
                dve.wait_ge(s_exp, vt + 1)
                dve.nop(nofuse=True)
                v.reciprocal(gate_sum[:, m:m + 1], gate_sum[:, m:m + 1])
                dve.drain()
                v.tensor_scalar(out=gate[:, m, :], in0=gate[:, m, :], scalar1=gate_sum[:, m:m + 1], scalar2=0.5,
                                op0=ALU.mult, op1=ALU.mult)

            def weigh(vt, m, tile, g):
                group = vt * GROUPS + g
                for i in range(GROUP):
                    k = g * GROUP + i
                    dve.wait_ge(s_slot[k % SLOTS], slot_filled(vt, k))
                    v.tensor_tensor_reduce(out=product[:, i % 2], in0=rows_of(k % SLOTS)[:, 0:D], in1=hn[:, tile],
                                           scale=1.0, scalar=0.0, op0=ALU.mult, op1=ALU.add,
                                           accum_out=dots[:, i:i + 1])
                    if i % 2:
                        dve.drain()
                x = dots[:, 0:GROUP]
                v.tensor_tensor(out=gl[:, 0, :], in0=x, in1=x, op=ALU.mult)
                v.tensor_tensor(out=gl[:, 1, :], in0=gate[:, m, g * GROUP:(g + 1) * GROUP], in1=x, op=ALU.mult)
                dve.drain()
                v.tensor_scalar(out=gl[:, 0, :], in0=gl[:, 0, :], scalar1=0.044715, scalar2=1.0, op0=ALU.mult,
                                op1=ALU.add)
                dve.drain()
                v.tensor_tensor(out=gl[:, 2, :], in0=gl[:, 0, :], in1=x, op=ALU.mult).then_inc(s_poly, 1)
                dve.wait_ge(s_tanh, group + 1)
                dve.nop(nofuse=True)
                v.scalar_tensor_tensor(out=weight[:, g % 2, :], in0=gl_tanh[:, :], scalar=1.0, in1=gl[:, 1, :],
                                       op0=ALU.add, op1=ALU.mult).then_inc(s_wt, 1)
                dve.drain()

            def add(vt, m, tile, rows=P):
                dve.wait_ge(s_used, (vt + 1) * TOPK)
                dve.nop(nofuse=True)
                total = ps[0:rows, 2 * (m % 2):2 * (m % 2) + 2, :].rearrange("p b n -> p (b n)")
                v.tensor_tensor(out=xs[0:rows, tile], in0=total, in1=xs[0:rows, tile], op=ALU.add).then_inc(s_acc, 1)
                dve.drain()

            def head_tile(vt, m, tile, before, ahead, rows=P):
                soft(vt, m)
                dve.drain()
                weigh(vt, m, tile, 0)
                add(vt - 1, m - 1, before, rows)
                rest = [lambda g=g: weigh(vt, m, tile, g) for g in range(1, GROUPS)]
                if ahead is None:
                    for group in rest:
                        group()
                else:
                    ahead()
                    choose((m + 2) % BUFS, (m + 2) % BUFS, rest)

            def prompt_head(head, first=0):
                for m in range(first, HT):
                    ahead = (lambda: later_scores(head + 1)) if m == 2 else (lambda: None)
                    head_tile(head * HT + m, m, m, (m - 1) % HT, ahead)

            dve.wait_ge(s_gain, 16)
            peer_norm(0)
            mix_add(2, 0)
            mix_add(3, 0)
            dve.wait_ge(s_retout, 32)
            first_scores(0)
            choose(0, 0, [lambda: peer_norm(1), lambda: mix_add(4, 0)])
            mix_add(2, 1)
            first_scores(1)
            peer_norm(2)
            mix_add(3, 1)
            soft(0, 0)
            dve.drain()
            weigh(0, 0, 0, 0)
            mix_add(4, 1)

            def second_group():
                peer_norm(3)
                weigh(0, 0, 0, 1)
            choose(1, 1, [second_group, lambda: first_scores(2)])

            def third_group():
                peer_norm(4)
                weigh(0, 0, 0, 2)
            choose(2, 2, [third_group, lambda: weigh(0, 0, 0, 3)])
            soft(1, 1)
            dve.drain()
            weigh(1, 1, 1, 0)
            add(0, 0, 0)
            first_scores(3)

            def third_group():
                first_scores(4)
                weigh(1, 1, 1, 2)
            weigh(1, 1, 1, 1)
            choose(3, 3, [third_group, lambda: weigh(1, 1, 1, 3)])
            soft(2, 2)
            dve.drain()
            weigh(2, 2, 2, 0)
            add(1, 1, 1)
            weigh(2, 2, 2, 1)
            later_scores(1)
            choose(0, 0, [lambda: weigh(2, 2, 2, 2), lambda: weigh(2, 2, 2, 3)])
            prompt_head(0, 3)
            with dve.Fori(1, PH - 1) as head:
                prompt_head(head)

            def turned_scores():
                dve.wait_ge(s_turned, 1)
                v.tensor_copy(scores[:, 0:2], ps[:, Q_BANKS, :].rearrange("p (s v n) -> p v s n", s=2, v=2))
                dve.drain()

            last = (PH - 1) * HT
            for m in range(HT):
                ahead = turned_scores if m == 2 else (lambda: None)
                head_tile(last + m, m, m, (m - 1) % HT, ahead)
            dve.wait_ge(s_rep, 16 * (FOLDED - 1))
            head_tile(VT - 2, 0, SAMPLE, SAMPLE - 1, None)
            head_tile(VT - 1, 1, SAMPLE, SAMPLE, None, DEC)

            def final_norm(t):
                r = ROWS[t]
                dve.wait_ge(s_rstd, 2 * TILES + t + 1)
                v.scalar_tensor_tensor(out=xs[0:r, t], in0=xs[0:r, t], scalar=rstd[0:r, 2 * TILES + t:2 * TILES + t + 1],
                                       in1=row_gain[0:r, :], op0=ALU.mult, op1=ALU.mult).then_inc(s_yout, 1)

            dve.wait_ge(s_gain2, 16)
            for t in range(SAMPLE):
                final_norm(t)
            add(VT - 1, 1, SAMPLE, DEC)
            final_norm(SAMPLE)

        @block.tensor
        def _(pe):
            mm = nc.tensor.matmul

            def open_bank(name):
                if name in BEFORE:
                    before, by = BEFORE[name]
                    pe.wait_ge(s_by[by], EMPTIED[before])
                return bank(name)

            def done(ins):
                ins.then_inc(s_pe, 1)

            def section(s):
                n = WEIGHT_ORDER.index(s)
                pe.wait_ge(s_w[n % WSLOTS], 16 * (n // WSLOTS + 1))
                return w_ring[:, n % WSLOTS]

            pe.wait_ge(s_ident, 16)

            def transposes(name, sources, r):
                out = open_bank(name)
                for j, src in enumerate(sources):
                    last = nc.tensor.transpose(out[:, j * P:j * P + r], src, ident[0:r, 0:r])
                done(last)

            def row_transposes(kind, t, i):
                transposes((kind, t, i), [hn[0:ROWS[t], t, k * P:(k + 1) * P] for k in range(4 * i, 4 * i + 4)],
                           ROWS[t])

            for t in range(TILES):
                pe.wait_ge(s_hn, t + 1)
                for i in range(2):
                    row_transposes("norm_t", t, i)
            pe.wait_ge(s_by["dve"], EMPTIED[("norm_t", SAMPLE, 1)])
            for s in (S_A, S_B):
                w = section(s)
                for c in range(CT):
                    out = open_bank(("glu", s, c))
                    for k in range(KD):
                        last = mm(out, w[:, k, c * P:(c + 1) * P], hT[:, k, 0:SEQ], start=k == 0, stop=k == KD - 1)
                    done(last)
                out = open_bank(("glu", s, CT))
                for c in range(CT):
                    for k in range(KD):
                        last = mm(out[:, c * DEC:(c + 1) * DEC], w[:, k, c * P:(c + 1) * P], hT[:, k, SEQ:T],
                                  start=k == 0, stop=k == KD - 1)
                last.then_inc(s_pe, 1)
                pe.drain().then_inc(s_wsec, 1)

            def rows_times(name, lhs, w, r, lo):
                out = open_bank(name)
                for k in range(KD):
                    last = mm(out[0:r, :], lhs[:, k, lo:lo + r], w[:, k, :], start=k == 0, stop=k == KD - 1)
                done(last)

            for s in (S_Q, S_K, S_G):
                w = section(s)
                for t in range(TILES):
                    rows_times(("qkvg", s, t), hT, w, ROWS[t], t * P)
                pe.drain().then_inc(s_wsec, 1)

            def channel_sums(kind, source):
                for i, (lo, hi) in enumerate(((0, SEQ), (SEQ, T))):
                    out = open_bank((kind, i))
                    for c in range(CT):
                        last = mm(out[:, 0:hi - lo], ones_cw[:, :], source[:, c, lo:hi], start=c == 0, stop=c == CT - 1)
                    done(last)

            def ret_step(kind, t):
                name = (kind, t)
                r = ROWS[t]
                v_rows = z[0:r, t, S_V].rearrange("p (h d) -> p h d", h=HEADS)
                if kind == "ret_qT":
                    pe.wait_ge(s_rot, t + 1)
                    transposes(name, [q_rot[0:r, h, :] for h in range(HEADS)], r)
                elif kind == "ret_kT":
                    transposes(name, [k_rot[0:r, h, :] for h in range(HEADS)], r)
                elif kind == "ret_scores":
                    pe.wait_ge(s_by["dve"], EMPTIED[("ret_kT", t)])
                    out = open_bank(name)
                    for h in range(HEADS):
                        last = mm(out[0:r, h * P:h * P + r], kT[:, h, 0:r], qT[:, h, 0:r], start=True, stop=True)
                    done(last)
                elif kind == "ret_out":
                    pe.wait_ge(s_by["dve"], EMPTIED[("ret_scores", t)])
                    pe.wait_ge(s_by["act"], EMPTIED[("qkvg", S_V, t)])
                    if 0 < t < SAMPLE:
                        pe.wait_ge(s_by["dve"], EMPTIED[("ret_state", t - 1)])
                    if t == SAMPLE:
                        pe.wait_ge(s_st, 32)
                    out = open_bank(name)
                    for h in range(HEADS):
                        part = out[0:r, h * HD:(h + 1) * HD]
                        last = mm(part, sc_dec[0:r, h, 0:r], v_rows[:, h, :], start=True, stop=t == 0)
                        if t:
                            last = mm(part, qT_cross[t % 2][:, h, 0:r], state[:, 1 if t == SAMPLE else 0, h, :],
                                      start=False, stop=True)
                    done(last)
                elif kind == "ret_state":
                    pe.wait_ge(s_kdec, t + 1)
                    out = open_bank(name)
                    for h in range(HEADS):
                        last = mm(out[:, h * HD:(h + 1) * HD], k_dec[0:r, h, :], v_rows[:, h, :], start=True, stop=True)
                    done(last)
                else:
                    pe.wait_ge(s_on, t + 1)
                    transposes(name, [o_norm[0:r, h, :] for h in range(HEADS)], r)

            w_out = []

            def mix_out(t, i):
                if not w_out:
                    w_out.extend([section(S_OUT), section(S_OUT + 1)])
                    pe.wait_ge(s_yconv, 1)
                if i == 0:
                    pe.wait_ge(s_by["dve"], EMPTIED[("ret_yT", t)])
                rows_times(("mix_out", t, i), yT, w_out[i], ROWS[t], t * P)
                if t == SAMPLE:
                    pe.drain().then_inc(s_wsec, 1)

            w = section(S_V)
            for name in retention_schedule():
                if name[0] == "qkvg":
                    t = name[2]
                    rows_times(name, hT, w, ROWS[t], t * P)
                    if t == SAMPLE:
                        pe.drain().then_inc(s_wsec, 1)
                elif name == ("ln_mean", 0):
                    pe.wait_ge(s_conv, 1)
                    channel_sums("ln_mean", conv)
                elif name == ("ln_var", 0):
                    pe.wait_ge(s_csq, CT)
                    channel_sums("ln_var", yT[:, HEADS:KD, :])
                elif name[0].startswith("ret_"):
                    ret_step(*name)
                elif name[0] == "mix_out":
                    mix_out(*name[1:])

            def sample_scores(out, queries, keys):
                for s in range(2):
                    last = mm(out[:, s * DEC:(s + 1) * DEC], keys[:, s, :], queries[:, s, SEQ:T], start=True, stop=True)
                return last

            def first_query(t):
                r = ROWS[t]
                pe.wait_ge(s_by["act"], EMPTIED[("ffn_t", t, 1)])
                out = open_bank(("query", t))
                for s in range(2):
                    for k in range(KD):
                        last = mm(out[:, s * P:s * P + r], head_w[0][0][:, k, s * KEYS:(s + 1) * KEYS],
                                  hT[:, k, t * P:t * P + r], start=k == 0, stop=k == KD - 1)
                done(last)

            def first_scores(t):
                pe.wait_ge(s_by["act"], EMPTIED[("query", t)])
                out = open_bank(("scores", t))
                keys = head_w[0][1]
                if t == SAMPLE:
                    done(sample_scores(out, queryT, keys))
                    return
                for s in range(2):
                    last = mm(out[:, s * KEYS:(s + 1) * KEYS], queryT[:, s, t * P:(t + 1) * P], keys[:, s, :],
                              start=True, stop=True)
                done(last)

            def later_query(head, i):
                weights = head_w[1][0]
                if isinstance(head, int) and head == 1:
                    pe.wait_ge(s_by["act"], EMPTIED[("query", SAMPLE)])
                    pe.wait_ge(s_by["dve"], EMPTIED[("scores", SAMPLE)])
                else:
                    pe.wait_ge(s_scored, (head - 2) * 3 + (i + 1))
                pe.wait_ge(s_hw[1], head * 16)
                pe.nop(nofuse=True)
                out = ps[:, Q_BANKS + i, :]
                if i < 2:
                    for k in range(KD):
                        last = mm(out, weights[:, k, i * KEYS:(i + 1) * KEYS], hT[:, k, 0:SEQ], start=k == 0,
                                  stop=k == KD - 1)
                else:
                    for s in range(2):
                        for k in range(KD):
                            last = mm(out[:, s * DEC:(s + 1) * DEC], weights[:, k, s * KEYS:(s + 1) * KEYS],
                                      hT[:, k, SEQ:T], start=k == 0, stop=k == KD - 1)
                last.then_inc(s_proj, 1)

            def later_scores(head):
                keys = head_w[1][1]
                for i in range(3):
                    pe.wait_ge(s_queries, (head - 1) * 3 + (i + 1))
                    pe.nop(nofuse=True)
                    out = ps[:, Q_BANKS + i, :]
                    if i < 2:
                        for t in range(HT):
                            last = mm(out[:, t * KEYS:(t + 1) * KEYS], queryT[:, i, t * P:(t + 1) * P], keys[:, i, :],
                                      start=True, stop=True)
                    else:
                        last = sample_scores(out, queryT, keys)
                    last.then_inc(s_proj, 1)

            def sum_up(vt, m, g):
                for k in range(g * GROUP, (g + 1) * GROUP):
                    pe.wait_ge(s_slot[k % SLOTS], slot_filled(vt, k))
                    pe.wait_ge(s_diag, vt * TOPK + (k + 1))
                    for half in range(2):
                        last = mm(ps[:, 2 * (m % 2) + half, :], diag[:, k % DIAGS, :],
                                  rows_of(k % SLOTS)[:, D + half * SEC:D + (half + 1) * SEC], start=k == 0,
                                  stop=k == TOPK - 1)
                    last.then_inc(s_used, 1)

            def head_tile(vt, m, behind={}):
                if not isinstance(vt, int) or vt >= 2:
                    pe.wait_ge(s_acc, vt - 1)
                    pe.nop(nofuse=True)
                for g in range(GROUPS):
                    sum_up(vt, m, g)
                    if g in behind:
                        behind[g]()

            def next_head(head, m):
                if m == 0:
                    return {1: lambda: later_query(head + 1, 0), 3: lambda: later_query(head + 1, 1)}
                if m == 1:
                    return {1: lambda: later_query(head + 1, 2), 2: lambda: later_scores(head + 1)}
                return {}

            for step in TRANSITION:
                if step[0] == "mix_out":
                    mix_out(*step[1:])
                elif step[0] == "ffn_t":
                    pe.wait_ge(s_hn, TILES + step[1] + 1)
                    row_transposes(*step)
                elif step[0] == "query":
                    if step[1] == 0:
                        pe.wait_ge(s_hw[0], 16)
                    first_query(step[1])
                elif step[0] == "scores":
                    first_scores(step[1])
                else:
                    if step[1:] == (0, 0):
                        pe.wait_ge(s_by["dve"], EMPTIED[("mix_out", SAMPLE, 1)])
                    sum_up(step[1], step[1], step[2])
            later_query(1, 0)
            sum_up(1, 1, 2)
            later_query(1, 1)
            sum_up(1, 1, 3)
            later_query(1, 2)
            head_tile(2, 2, {0: lambda: later_scores(1)})
            head_tile(3, 3)
            with pe.Fori(1, PH - 1) as head:
                for m in range(HT):
                    head_tile(head * HT + m, m, next_head(head, m))

            def turn_scores():
                pe.wait_ge(s_scored, (PH - 1) * 3)
                for i in range(4):
                    last = nc.tensor.transpose(ps[:, Q_BANKS, i * P:(i + 1) * P], sampleT[:, i * P:(i + 1) * P],
                                               ident[:, :])
                last.then_inc(s_turned, 1)

            for vt in range((PH - 1) * HT, VT):
                head_tile(vt, vt % BUFS)
                if vt == (PH - 1) * HT:
                    turn_scores()


_INS = ["x_prompt", "x_sample", "state_ret", "conv_state", "weights", "head_weights", "params", "consts", "gain_ffn",
        "gain_final", "experts"]
_OUTS = [("y_prompt", (SEQ, D)), ("y_sample", (DEC, D)), ("ret_prompt", (P, HEADS, HD)), ("ret_sample", (P, HEADS, HD)),
         ("conv_prompt", (P, CT, PAD)), ("conv_sample", (P, CT, PAD))]


def lay_out(inputs):
    a = {k: np.asarray(v) for k, v in inputs.items()}
    w_all = np.concatenate([a["w_in"][0], a["w_out"][0]], axis=1)
    weights = w_all.reshape(KD, P, SECTIONS, SEC).transpose(2, 1, 0, 3)

    queries = a["peer_query"][0].reshape(KD, P, PH, 2 * KEYS).transpose(2, 1, 0, 3).reshape(PH, P, HEAD_W)
    keys = a["peer_sub_keys"][0].transpose(0, 3, 1, 2).reshape(PH, P, 2 * KEYS)

    def columns(x):
        return x.reshape(-1, P).T
    taps = a["conv_dw"][0].reshape(TAPS, CT, P).transpose(2, 1, 0).reshape(P, CT * TAPS)
    params = np.concatenate([columns(a["norm_mix"][0]), columns(a["ret_gn_gain"][0]), columns(a["conv_dw_bias"][0]),
                             columns(a["conv_ln_gain"][0]), columns(a["conv_ln_bias"][0]), taps], axis=1)
    out = {
        "x_prompt": a["x_prompt"][0], "x_sample": a["x_sample"][0],
        "state_ret": a["state_retention"][0, 0].transpose(1, 0, 2),
        "conv_state": a["state_conv"][0, 0].reshape(PAD, CT, P).transpose(2, 1, 0),
        "weights": weights,
        "head_weights": np.concatenate([queries, keys], axis=2),
        "params": params, "consts": shape_constants(),
        "gain_ffn": a["norm_ffn"], "gain_final": a["norm_final"][None, :],
        "experts": np.concatenate([a["peer_down"][0], a["peer_up"][0]], axis=1),
    }
    return {k: np.ascontiguousarray(v) for k, v in out.items()}


def program(nc, arrays):
    args = [nc.dram_tensor(n, arrays[n].shape, FP32, kind="ExternalInput").ap() for n in _INS]
    args += [nc.dram_tensor(n, shape, FP32, kind="ExternalOutput").ap() for n, shape in _OUTS]
    build(nc, *args)
    return nc


def kernel(**inputs):
    import concourse.bacc as bacc
    from concourse.bass_utils import run_bass_kernel_spmd
    arrays = lay_out(inputs)
    nc = program(bacc.Bacc("TRN2", target_bir_lowering=False, num_devices=1), arrays)
    r = run_bass_kernel_spmd(nc, [arrays], core_ids=[0]).results[0]
    ret = [r[n].transpose(1, 0, 2)[None, None] for n in ("ret_prompt", "ret_sample")]
    conv = [r[n].transpose(2, 1, 0).reshape(1, 1, PAD, CW) for n in ("conv_prompt", "conv_sample")]
    return (r["y_prompt"][None], r["y_sample"][None], ret[0], ret[1], conv[0], conv[1])
```
